# Optimizing a Trainium2 kernel written in Bass

```python
import jax, jax.numpy as jnp
from jax import lax
import numpy as np

D_MODEL = 1024
BATCH = 1
SEQ = 4096
DEPTH = 1

CHUNK = 64
HEAD_DIM = 64
D_MIX = D_MODEL
ATTN_HEADS = 8
KV_HEADS = 2
ATTN_WIDTH = ATTN_HEADS * HEAD_DIM
KV_WIDTH = KV_HEADS * HEAD_DIM
GMLP_GROUPS = 8
GMLP_GROUP_DIM = (D_MIX - ATTN_WIDTH) // GMLP_GROUPS
GMLP_WIDTH = GMLP_GROUPS * GMLP_GROUP_DIM
GMLP_BLOCK = 128
WINDOW = 128
WINDOW_CHUNKS = WINDOW // CHUNK
ROPE_THETA = 500000.0
ROT_DIM = HEAD_DIM // 4
N_EXPERT_GROUPS = 4
EXPERTS_PER_GROUP = 8
N_EXPERTS = N_EXPERT_GROUPS * EXPERTS_PER_GROUP
TOP_K_IN_GROUP = 2
D_EXPERT = 512
MOE_BLOCK = 128
D_IN = ATTN_WIDTH + 2 * KV_WIDTH + 2 * GMLP_WIDTH
EPS = 1e-6

kernel_name = "hymba_swa_sink_gmlp_hiermoe_block"

def rms_norm(t, g):
    tf = t.astype(jnp.float32)
    y = tf * lax.rsqrt(jnp.mean(tf * tf, axis=-1, keepdims=True) + EPS)
    return (y * g.astype(jnp.float32)).astype(t.dtype)

def layer_norm(t, g, b):
    tf = t.astype(jnp.float32)
    mu = jnp.mean(tf, axis=-1, keepdims=True)
    var = jnp.mean(jnp.square(tf - mu), axis=-1, keepdims=True)
    y = (tf - mu) * lax.rsqrt(var + EPS)
    return (y * g.astype(jnp.float32) + b.astype(jnp.float32)).astype(t.dtype)

def rope_tables(S):
    pos = jnp.arange(S, dtype=jnp.float32)
    inv_freq = ROPE_THETA ** (-jnp.arange(0, ROT_DIM, 2, dtype=jnp.float32) / ROT_DIM)
    ang = pos[:, None] * inv_freq[None, :]
    return jnp.cos(ang), jnp.sin(ang)

def apply_partial_rope(t, cos, sin):
    half = ROT_DIM // 2
    r1 = t[..., :half].astype(jnp.float32)
    r2 = t[..., half:ROT_DIM].astype(jnp.float32)
    c = cos[None, :, None, :]
    s = sin[None, :, None, :]
    rot = jnp.concatenate([r1 * c - r2 * s, r2 * c + r1 * s], axis=-1).astype(t.dtype)
    return jnp.concatenate([rot, t[..., ROT_DIM:]], axis=-1)

def window_sink_attention(q, k, v, sinks):
    B, S, H, D = q.shape
    nc = S // CHUNK
    grp = H // KV_HEADS
    qc = q.reshape(B, nc, CHUNK, KV_HEADS, grp, D)
    kc = k.reshape(B, nc, CHUNK, KV_HEADS, D)
    vc = v.reshape(B, nc, CHUNK, KV_HEADS, D)

    def band(t):
        parts = [jnp.pad(t, ((0, 0), (w, 0), (0, 0), (0, 0), (0, 0)))[:, :nc]
                 for w in range(WINDOW_CHUNKS - 1, -1, -1)]
        return jnp.concatenate(parts, axis=2)

    kb, vb = band(kc), band(vc)
    lag = jnp.repeat(jnp.arange(WINDOW_CHUNKS - 1, -1, -1), CHUNK)
    valid = (jnp.arange(nc)[:, None] - lag[None, :]) >= 0
    s = jnp.einsum('bnqkgd,bnskd->bnkgqs', qc, kb).astype(jnp.float32) * (D ** -0.5)
    s = jnp.where(valid[None, :, None, None, None, :], s, -jnp.inf)
    sink = jnp.broadcast_to(sinks.astype(jnp.float32).reshape(KV_HEADS, grp)[None, None, :, :, None, None],
                            s.shape[:-1] + (1,))
    p = jax.nn.softmax(jnp.concatenate([s, sink], axis=-1), axis=-1)[..., :-1]
    o = jnp.einsum('bnkgqs,bnskd->bnqkgd', p.astype(v.dtype), vb)
    return o.reshape(B, S, H * D)

def chunked_spatial_gating(u, v, w_s, b_s, ln_g, ln_b):
    B, S, _ = u.shape
    nb = S // GMLP_BLOCK
    u = jax.nn.gelu(u).reshape(B, nb, GMLP_BLOCK, GMLP_GROUPS, GMLP_GROUP_DIM)
    v = jax.nn.gelu(v).reshape(B, nb, GMLP_BLOCK, GMLP_GROUPS, GMLP_GROUP_DIM)
    v = layer_norm(v, ln_g, ln_b)
    cidx = jnp.arange(GMLP_BLOCK) // CHUNK
    mask = cidx[None, :] <= cidx[:, None]
    w = jnp.where(mask[None], w_s, 0)
    sg = jnp.einsum('gij,bnjgc->bnigc', w, v) + b_s.T[None, None, :, :, None]
    return (u * sg).reshape(B, S, GMLP_WIDTH)

def hierarchical_moe(x, w_rg, b_rg, w_re, b_re, w_gate, w_up, w_down):
    T, D = x.shape
    xf = x.astype(jnp.float32)
    g_prob = jax.nn.softmax(xf @ w_rg.astype(jnp.float32) + b_rg.astype(jnp.float32), axis=-1)
    g_p, g_idx = lax.top_k(g_prob, 1)
    e_logits = (xf @ w_re.astype(jnp.float32) + b_re.astype(jnp.float32)).reshape(T, N_EXPERT_GROUPS, EXPERTS_PER_GROUP)
    sel = jax.nn.one_hot(g_idx[:, 0], N_EXPERT_GROUPS, dtype=jnp.float32)
    e_sel = jnp.einsum('tge,tg->te', e_logits, sel)
    top_l, top_i = lax.top_k(e_sel, TOP_K_IN_GROUP)
    weights = g_p * jax.nn.softmax(top_l, axis=-1)
    expert_id = g_idx * EXPERTS_PER_GROUP + top_i

    A = T * TOP_K_IN_GROUP
    flat_e = expert_id.reshape(A).astype(jnp.int32)
    flat_w = weights.reshape(A)
    flat_t = jnp.repeat(jnp.arange(T, dtype=jnp.int32), TOP_K_IN_GROUP)
    order = jnp.argsort(flat_e)
    se = flat_e[order]
    counts = jnp.bincount(flat_e, length=N_EXPERTS)
    padded = (counts + MOE_BLOCK - 1) // MOE_BLOCK * MOE_BLOCK
    start = jnp.cumsum(counts) - counts
    pstart = jnp.cumsum(padded) - padded
    dest = pstart[se] + jnp.arange(A, dtype=jnp.int32) - start[se]
    cap = A + N_EXPERTS * MOE_BLOCK
    nblk = cap // MOE_BLOCK
    tok_buf = jnp.full((cap,), T, dtype=jnp.int32).at[dest].set(flat_t[order])
    w_buf = jnp.zeros((cap,), x.dtype).at[dest].set(flat_w[order].astype(x.dtype))
    x_buf = jnp.concatenate([x, jnp.zeros((1, D), x.dtype)], axis=0)[tok_buf]
    blk_e = jnp.clip(jnp.searchsorted(jnp.cumsum(padded), jnp.arange(nblk) * MOE_BLOCK, side='right'),
                     0, N_EXPERTS - 1)

    def run_block(args):
        xb, e = args
        hdn = jax.nn.silu(xb @ w_gate[e]) * (xb @ w_up[e])
        return hdn @ w_down[e]

    y = lax.map(run_block, (x_buf.reshape(nblk, MOE_BLOCK, D), blk_e)).reshape(cap, D)
    y = y * w_buf[:, None]
    return jnp.zeros((T + 1, D), x.dtype).at[tok_buf].add(y)[:T]

def setup_inputs(seed: int = 0) -> dict:
    key = jax.random.key(seed)
    ks = jax.random.split(key, 24)
    f = jnp.float32
    nrm = lambda k, shape, scale: jax.random.normal(k, shape, f) * scale
    L = DEPTH
    return {
        "x": nrm(ks[0], (BATCH, SEQ, D_MODEL), 1.0),
        "g_mix_norm": 1.0 + nrm(ks[1], (L, D_MODEL), 0.05),
        "w_in": nrm(ks[2], (L, D_MODEL, D_IN), D_MODEL ** -0.5),
        "b_in": nrm(ks[3], (L, D_IN), 0.02),
        "sinks": nrm(ks[4], (L, ATTN_HEADS), 1.0),
        "gmlp_w_s": nrm(ks[5], (L, GMLP_GROUPS, GMLP_BLOCK, GMLP_BLOCK), GMLP_BLOCK ** -0.5),
        "gmlp_b_s": 1.0 + nrm(ks[6], (L, GMLP_GROUPS, GMLP_BLOCK), 0.1),
        "gmlp_ln_g": 1.0 + nrm(ks[7], (L, GMLP_GROUPS, GMLP_GROUP_DIM), 0.05),
        "gmlp_ln_b": nrm(ks[8], (L, GMLP_GROUPS, GMLP_GROUP_DIM), 0.02),
        "g_attn_out": 1.0 + nrm(ks[9], (L, ATTN_WIDTH), 0.05),
        "g_gmlp_out": 1.0 + nrm(ks[10], (L, GMLP_WIDTH), 0.05),
        "w_out": nrm(ks[11], (L, D_MIX, D_MODEL), D_MIX ** -0.5),
        "g_ffn_norm": 1.0 + nrm(ks[12], (L, D_MODEL), 0.05),
        "w_router_group": nrm(ks[13], (L, D_MODEL, N_EXPERT_GROUPS), D_MODEL ** -0.5),
        "b_router_group": nrm(ks[14], (L, N_EXPERT_GROUPS), 0.01),
        "w_router_expert": nrm(ks[15], (L, D_MODEL, N_EXPERTS), D_MODEL ** -0.5),
        "b_router_expert": nrm(ks[16], (L, N_EXPERTS), 0.01),
        "w_gate": nrm(ks[17], (L, N_EXPERTS, D_MODEL, D_EXPERT), D_MODEL ** -0.5),
        "w_up": nrm(ks[18], (L, N_EXPERTS, D_MODEL, D_EXPERT), D_MODEL ** -0.5),
        "w_down": nrm(ks[19], (L, N_EXPERTS, D_EXPERT, D_MODEL), D_EXPERT ** -0.5),
        "g_final": 1.0 + nrm(ks[20], (D_MODEL,), 0.05),
    }

def reference(x, g_mix_norm, w_in, b_in, sinks, gmlp_w_s, gmlp_b_s, gmlp_ln_g, gmlp_ln_b,
              g_attn_out, g_gmlp_out, w_out, g_ffn_norm, w_router_group, b_router_group,
              w_router_expert, b_router_expert, w_gate, w_up, w_down, g_final):
    B, S, D = x.shape
    cos, sin = rope_tables(S)
    splits = [ATTN_WIDTH, ATTN_WIDTH + KV_WIDTH, ATTN_WIDTH + 2 * KV_WIDTH,
              ATTN_WIDTH + 2 * KV_WIDTH + GMLP_WIDTH]
    h = x
    for l in range(DEPTH):
        hn = rms_norm(h, g_mix_norm[l])
        z = hn @ w_in[l] + b_in[l]
        q, k, v, gu, gv = jnp.split(z, splits, axis=-1)
        q = apply_partial_rope(q.reshape(B, S, ATTN_HEADS, HEAD_DIM), cos, sin)
        k = apply_partial_rope(k.reshape(B, S, KV_HEADS, HEAD_DIM), cos, sin)
        v = v.reshape(B, S, KV_HEADS, HEAD_DIM)
        a_out = window_sink_attention(q, k, v, sinks[l])
        m_out = chunked_spatial_gating(gu, gv, gmlp_w_s[l], gmlp_b_s[l], gmlp_ln_g[l], gmlp_ln_b[l])
        mix = jnp.concatenate([rms_norm(a_out, g_attn_out[l]), rms_norm(m_out, g_gmlp_out[l])], axis=-1)
        h = h + mix @ w_out[l]
        hn = rms_norm(h, g_ffn_norm[l]).reshape(B * S, D)
        ff = hierarchical_moe(hn, w_router_group[l], b_router_group[l], w_router_expert[l],
                              b_router_expert[l], w_gate[l], w_up[l], w_down[l])
        h = h + ff.reshape(B, S, D)
    return rms_norm(h, g_final)


_drawn_inputs = setup_inputs


def setup_inputs(seed=0):
    import zlib

    import numpy as np

    out = dict(_drawn_inputs(seed))
    spreads = {}
    factors = {'sinks': 4.955, 'gmlp_ln_b': 4.222, 'b_router_group': 4.913, 'b_router_expert': 4.997}
    for name, (base, spread) in spreads.items():
        noise = np.random.default_rng([zlib.crc32(name.encode()), seed]).standard_normal(out[name].shape)
        drawn = base * np.exp(spread * noise) if base else spread * noise
        out[name] = __import__('jax').numpy.asarray(drawn.astype(out[name].dtype))
    for name, factor in factors.items():
        out[name] = (out[name] * factor).astype(out[name].dtype)
    return out
```

```python
from contextlib import ExitStack

import numpy as np
import concourse.bass as bass
from concourse import mybir

F32 = mybir.dt.float32
F32R = mybir.dt.float32r
BF16 = mybir.dt.bfloat16
I32 = mybir.dt.int32
U32 = mybir.dt.uint32
ACT = mybir.ActivationFunctionType
ALU = mybir.AluOpType
X = mybir.AxisListType.X

P = 128
SEQ = 4096
D = 1024
NT = SEQ // P
KT = D // P
CHUNK = 64
HD = 64
HEADS = 8
KVH = 2
GRP = HEADS // KVH
ROT = HD // 4
AW = HEADS * HD
KVW = KVH * HD
GG = 8
GC = 64
GW = GG * GC
DIN = AW + 2 * KVW + 2 * GW
V0 = AW + KVW
G0 = AW + 2 * KVW
ZC = [(0, AW), (AW, G0), (G0, G0 + GW), (G0 + GW, DIN)]
NG = 4
EPG = 8
NE = NG * EPG
F = 512
FT = F // P
BLK = 128
EPS = 1e-6
GELU_C = 0.7978845608028654
ROWS_PER_EXPERT = SEQ
MAXB = 2 * NE + 2 * SEQ // BLK + 2
ENTRY = 4


def makers(ctx, nc, phase):
    return (lambda n, s, d=F32: ctx.enter_context(nc.sbuf_tensor(f"{phase}_{n}", s, d)),
            lambda n, s: ctx.enter_context(nc.psum_tensor(f"{phase}_{n}", s, F32)),
            lambda n: ctx.enter_context(nc.semaphore(f"{phase}_{n}")))


def mixers(nc, x, w_in, b_in, sinks, w_s, b_s, ln_g, ln_b, g_mix, mats, rope, mix_dram):
    with ExitStack() as ctx:
        sb, pb, sem = makers(ctx, nc, "mixers")

        w_hi = sb("w_hi", [P, KT, DIN], F32R)
        w_lo = sb("w_lo", [P, KT, DIN], BF16)
        w_raw = [sb(f"w_raw{s}", [P, DIN]) for s in range(2)]
        gmix = sb("gmix", [P, KT])
        bias = sb("bias", [P, DIN])
        ident = sb("ident", [P, P])
        rope_sb = sb("rope_sb", [P, NT, 2, ROT])
        sink = sb("sink", [P, HEADS])
        ws_raw = sb("ws_raw", [P, GG, P])
        wsT = sb("wsT", [P, GG, P])
        bs_sb = sb("bs_sb", [P, GG])
        lng = sb("lng", [P, GW])
        lnb = sb("lnb", [P, GW])
        gate_bias = sb("gate_bias", [P, GW])
        xt = sb("xt", [P, D])
        sq_junk = sb("sq_junk", [P, D])
        ssq = sb("ssq", [P, 1])
        rstd = sb("rstd", [P, 1])
        xT_hi = sb("xT_hi", [P, KT, P], F32R)
        xT_lo = sb("xT_lo", [P, KT, P], F32R)
        xT_b = sb("xT_b", [P, KT, P], BF16)
        z = sb("z", [P, DIN])
        rot1 = sb("rot1", [P, HEADS + KVH, ROT])
        rot2 = sb("rot2", [P, HEADS + KVH, ROT])
        qT = sb("qT", [P, GRP, P])
        kT_cur = sb("kT_cur", [P, P])
        kT_mix = sb("kT_mix", [P, P])
        v_cur = sb("v_cur", [P, KVH, HD + 1])
        v_mix = sb("v_mix", [P, KVH, HD + 1])
        probs = sb("probs", [P, HEADS, P])
        probsT = sb("probsT", [P, HEADS, P])
        mx = sb("mx", [P, HEADS])
        neg_mx = sb("neg_mx", [P, HEADS])
        sink_d = sb("sink_d", [P, HEADS])
        sink_e = sb("sink_e", [P, HEADS])
        den = sb("den", [P, HEADS])
        gel = sb("gel", [P, 2 * GW])
        uv = sb("uv", [P, 2 * GW])
        vsq = sb("vsq", [P, GW])
        st8 = sb("st8", [P, GG])
        mean8 = sb("mean8", [P, GG])
        var8 = sb("var8", [P, GG])
        mix = sb("mix", [P, D])
        nss = sb("nss", [P, 2])
        nrs = sb("nrs", [P, 2])
        minus_half = sb("minus_half", [P, GG])

        ps_z = [pb(f"ps_z{i}", [P, 512]) for i in range(2)]
        ps_t = pb("ps_t", [P, KT, P])
        ps_s = pb("ps_s", [P, HEADS, P])
        ps_o = pb("ps_o", [P, 2, 512])

        ld_w = [sem(f"ld_w{s}") for s in range(2)]
        ld_small = sem("ld_small")
        ld_x = sem("ld_x")
        st_mix = sem("st_mix")
        a_whi = sem("a_whi")
        v_wlo = sem("v_wlo")
        pe_wsT = sem("pe_wsT")
        v_wsT = sem("v_wsT")
        pe_gb = sem("pe_gb")
        v_init = sem("v_init")
        pe_xt = sem("pe_xt")
        pe_z = sem("pe_z")
        pe_qk = sem("pe_qk")
        pe_s = sem("pe_s")
        pe_pt = sem("pe_pt")
        pe_pv = sem("pe_pv")
        pe_sg = sem("pe_sg")
        a_ssq = sem("a_ssq")
        a_xh = sem("a_xh")
        a_gsq = sem("a_gsq")
        a_tanh = sem("a_tanh")
        a_vsq = sem("a_vsq")
        a_exp = sem("a_exp")
        a_pt = sem("a_pt")
        a_qt = sem("a_qt")
        a_nsq = sem("a_nsq")
        a_mix = sem("a_mix")
        v_xl = sem("v_xl")
        v_z = sem("v_z")
        v_rope = sem("v_rope")
        v_kt = sem("v_kt")
        v_vv = sem("v_vv")
        v_gp = sem("v_gp")
        v_cen = sem("v_cen")
        v_max = sem("v_max")
        v_vn = sem("v_vn")
        v_o = sem("v_o")
        v_var = sem("v_var")
        pe_held = sem("pe_held")
        p_held = sem("p_held")
        p_rstd = sem("p_rstd")
        p_var = sem("p_var")
        p_nrs = sem("p_nrs")

        x_t = x.rearrange("b (t p) d -> (b t) p d", p=P)
        mix_t = mix_dram.rearrange("(t p) d -> t p d", p=P)
        w_in_t = w_in.rearrange("l (k p) n -> (l k) p n", p=P)
        N_SMALL = 9

        block = ctx.enter_context(nc.Block())

        @block.sync
        def _(sp):
            sp.dma_start(xt[:], x_t[0]).then_inc(ld_x, 16)
            sp.dma_start(ident[:], mats[:, 0:P]).then_inc(ld_small, 16)
            sp.dma_start(gmix[:], g_mix.rearrange("l (k p) -> p (l k)", p=P),
                         allow_slow_non_contiguous=True).then_inc(ld_small, 16)
            for k in range(KT):
                if k >= 2:
                    sp.wait_ge(v_wlo, k - 1)
                sp.dma_start(w_raw[k % 2][:], w_in_t[k]).then_inc(ld_w[k % 2], 16)
                if k == 1:
                    sp.dma_start(bias[:], b_in.to_broadcast((P, DIN))).then_inc(ld_small, 16)
                    sp.dma_start(rope_sb[:].rearrange("p t a c -> p t (a c)"),
                                 rope.rearrange("(t p) c -> p t c", p=P)).then_inc(ld_small, 16)
                    sp.dma_start(sink[:], sinks.to_broadcast((P, HEADS))).then_inc(ld_small, 16)
                    sp.dma_start(ws_raw[:], w_s.rearrange("l g i j -> i (l g) j")).then_inc(ld_small, 16)
                    sp.dma_start(bs_sb[:], b_s.rearrange("l g i -> i (l g)"), allow_slow_non_contiguous=True).then_inc(ld_small, 16)
                    sp.dma_start(lng[:], ln_g.rearrange("l g c -> l (g c)").to_broadcast((P, GW))).then_inc(ld_small, 16)
                    sp.dma_start(lnb[:], ln_b.rearrange("l g c -> l (g c)").to_broadcast((P, GW))).then_inc(ld_small, 16)

            def load_x(n):
                sp.wait_ge(pe_xt, n)
                sp.wait_ge(a_ssq, n)
                sp.dma_start(xt[:], x_t[bass.ds(n, 1)].rearrange("a p d -> (a p) d")).then_inc(ld_x, 16)

            def store_mix(m):
                sp.wait_ge(a_mix, m + 1)
                sp.dma_start(mix_t[bass.ds(m, 1)].rearrange("a p d -> (a p) d"), mix[:]).then_inc(st_mix, 16)

            load_x(1)
            load_x(2)
            load_x(3)
            store_mix(0)
            with sp.Fori(2, NT - 2) as i:
                load_x(i + 2)
                store_mix(i - 1)
            store_mix(NT - 3)
            store_mix(NT - 2)
            store_mix(NT - 1)
            sp.wait_ge(st_mix, 16 * NT)

        @block.tensor
        def _(pe):
            def x_transposes(n, prior_qk):
                pe.wait_ge(ld_x, 16 * (n + 1))
                if prior_qk:
                    pe.wait_ge(a_qt, n - 1)
                    pe.wait_ge(v_kt, n - 1)
                for k in range(KT):
                    last = nc.tensor.transpose(ps_t[:, k, :], xt[:, k * P:(k + 1) * P], ident[:])
                last.then_inc(pe_xt, 1)

            def z_chunk(i, c, reused):
                if c == 0:
                    pe.wait_ge(v_xl, i + 1)
                if reused:
                    pe.wait_ge(v_z, 4 * i + c - 1)
                a, b = ZC[c]
                out = ps_z[c % 2][:, 0:b - a]
                for k in range(KT):
                    nc.tensor.matmul(out, xT_hi[:, k, :], w_hi[:, k, a:b], start=(k == 0), stop=False)
                    nc.tensor.matmul(out, xT_lo[:, k, :], w_hi[:, k, a:b], start=False, stop=False)
                    last = nc.tensor.matmul(out, xT_b[:, k, :], w_lo[:, k, a:b], start=False, stop=(k == KT - 1))
                last.then_inc(pe_z, 1)

            def scores(m, first):
                pe.wait_ge(a_qt, m + 1)
                pe.wait_ge(v_kt, m + 1)
                if not first:
                    pe.wait_ge(v_o, m)
                pe.sem_inc(pe_held, 1)
                for h in range(HEADS):
                    rows = slice(HD * (h // GRP), HD * (h // GRP) + HD)
                    for c, keys in ((0, kT_mix), (1, kT_cur)):
                        last = nc.tensor.matmul(ps_s[c * CHUNK:(c + 1) * CHUNK, h, :],
                                                qT[rows, h % GRP, c * CHUNK:(c + 1) * CHUNK], keys[rows, :],
                                                start=True, stop=True)
                last.then_inc(pe_s, 1)

            def prob_transposes(m):
                pe.wait_ge(a_exp, m + 1)
                for h in range(HEADS):
                    last = nc.tensor.transpose(ps_s[:, h, :], probs[:, h, :], ident[:])
                last.then_inc(pe_pt, 1)

            def attend(m):
                pe.wait_ge(a_pt, m + 1)
                pe.wait_ge(v_vv, m + 1)
                for h in range(HEADS):
                    o = (h % GRP) * (HD + 1)
                    for c, vals in ((0, v_mix), (1, v_cur)):
                        last = nc.tensor.matmul(ps_o[c * CHUNK:(c + 1) * CHUNK, h // GRP, o:o + HD + 1],
                                                probsT[:, h, c * CHUNK:(c + 1) * CHUNK], vals[:, h // GRP, :],
                                                start=True, stop=True)
                last.then_inc(pe_pv, 1)

            def gating(m):
                pe.wait_ge(v_vn, m + 1)
                for g in range(GG):
                    last = nc.tensor.matmul(ps_s[:, g // 2, (g % 2) * GC:(g % 2 + 1) * GC], wsT[:, g, :],
                                            uv[:, GW + g * GC:GW + (g + 1) * GC], start=True, stop=True)
                last.then_inc(pe_sg, 1)

            def qk_transposes(i, prior_x):
                pe.wait_ge(v_rope, i + 1)
                if prior_x:
                    pe.wait_ge(v_xl, i + 2)
                for b in range(GRP):
                    nc.tensor.transpose(ps_t[:, b, :], z[:, b * P:(b + 1) * P], ident[:])
                nc.tensor.transpose(ps_t[:, GRP, :], z[:, AW:AW + KVW], ident[:]).then_inc(pe_qk, 1)

            def step(i, a, b, nx, first, second):
                if a:
                    z_chunk(i, 0, not first)
                if b:
                    scores(i - 1, second)
                if a:
                    z_chunk(i, 1, not first)
                    z_chunk(i, 2, True)
                if b:
                    prob_transposes(i - 1)
                if nx:
                    x_transposes(i + 1, not first)
                if a:
                    z_chunk(i, 3, True)
                if b:
                    attend(i - 1)
                    gating(i - 1)
                if a:
                    qk_transposes(i, nx)

            pe.wait_ge(ld_small, 16 * N_SMALL)
            for g in range(GG):
                last = nc.tensor.transpose(ps_s[:, g, :], ws_raw[:, g, :], ident[:])
            last.then_inc(pe_wsT, 1)
            x_transposes(0, False)
            pe.wait_ge(v_wsT, 1)
            for g in range(GG):
                last = nc.tensor.matmul(ps_s[:, g // 2, (g % 2) * GC:(g % 2 + 1) * GC], wsT[:, g, :],
                                        lnb[:, g * GC:(g + 1) * GC], start=True, stop=True)
            last.then_inc(pe_gb, 1)
            pe.wait_ge(v_init, 1)
            pe.wait_ge(v_wlo, KT)
            step(0, True, False, True, True, False)
            step(1, True, True, True, False, True)
            with pe.Fori(2, NT - 1) as i:
                step(i, True, True, True, False, False)
            step(NT - 1, True, True, False, False, False)
            step(NT, False, True, False, False, False)

        @block.scalar
        def _(act):
            def square_x(n, first):
                act.wait_ge(ld_x, 16 * (n + 1))
                if not first:
                    act.wait_ge(p_rstd, n)
                nc.scalar.activation(sq_junk[:], xt[:], ACT.Square, accum_out=ssq[:]).then_inc(a_ssq, 1)

            def split_x(n, first):
                if not first:
                    act.wait_ge(pe_z, 4 * n)
                act.wait_ge(pe_xt, n + 1)
                nc.scalar.copy(xT_hi[:], ps_t[:]).then_inc(a_xh, 1)

            def step(i, a, b, nx, second):
                m = i - 1
                if b:
                    act.wait_ge(v_z, 4 * m + 4)
                    if not second:
                        act.wait_ge(v_cen, m)
                    nc.scalar.activation(gel[:], z[:, G0:DIN], ACT.Square).then_inc(a_gsq, 1)
                    act.wait_ge(v_gp, m + 1)
                    nc.scalar.activation(gel[:], gel[:], ACT.Tanh, scale=GELU_C).then_inc(a_tanh, 1)
                    act.wait_ge(v_cen, m + 1)
                    nc.scalar.activation(vsq[:], uv[:, GW:2 * GW], ACT.Square).then_inc(a_vsq, 1)
                    act.wait_ge(v_max, m + 1)
                    for h in range(HEADS):
                        nc.scalar.activation(probs[:, h, :], ps_s[:, h, :], ACT.Exp, bias=neg_mx[:, h:h + 1])
                    nc.scalar.activation(sink_e[:], sink_d[:], ACT.Exp).then_inc(a_exp, 1)
                    act.wait_ge(pe_pt, m + 1)
                    nc.scalar.copy(probsT[:], ps_s[:]).then_inc(a_pt, 1)
                if nx:
                    square_x(i + 1, False)
                    split_x(i + 1, False)
                if a:
                    act.wait_ge(pe_qk, i + 1)
                    nc.scalar.mul(qT[:], ps_t[:, 0:GRP, :], HD ** -0.5).then_inc(a_qt, 1)
                if b:
                    act.wait_ge(v_o, m + 1)
                    nc.scalar.activation(sq_junk[:, 0:AW], mix[:, 0:AW], ACT.Square, accum_out=nss[:, 0:1])
                    nc.scalar.activation(sq_junk[:, AW:D], mix[:, AW:D], ACT.Square, accum_out=nss[:, 1:2]).then_inc(a_nsq, 1)
                    act.wait_ge(p_nrs, m + 1)
                    nc.scalar.mul(mix[:, 0:AW], mix[:, 0:AW], nrs[:, 0:1])
                    nc.scalar.mul(mix[:, AW:D], mix[:, AW:D], nrs[:, 1:2]).then_inc(a_mix, 1)

            act.wait_ge(ld_small, 16 * N_SMALL)
            for k in range(KT):
                act.wait_ge(ld_w[k % 2], 16 * (k // 2 + 1))
                nc.scalar.mul(w_hi[:, k, :], w_raw[k % 2][:], gmix[:, k:k + 1]).then_inc(a_whi, 1)
            square_x(0, True)
            split_x(0, True)
            step(0, True, False, True, False)
            step(1, True, True, True, True)
            with act.Fori(2, NT - 1) as i:
                step(i, True, True, True, False)
            step(NT - 1, True, True, False, False)
            step(NT, False, True, False, False)

        @block.vector
        def _(dve):
            V = nc.vector

            def split_x(n, first):
                dve.wait_ge(a_xh, n + 1)
                if not first:
                    dve.wait_ge(pe_z, 4 * n)
                V.tensor_copy(xT_b[:], xT_hi[:].bitcast(F32))
                V.tensor_tensor(xT_lo[:], ps_t[:], xT_hi[:].bitcast(F32), ALU.subtract).then_inc(v_xl, 1)

            def z_chunk(i, c):
                dve.wait_ge(pe_z, 4 * i + c + 1)
                a, b = ZC[c]
                if c == 0:
                    placed = z[:, 0:AW].rearrange("p (h k d) -> p k h d", k=KVH, d=HD)
                    for kv in range(KVH):
                        cols = slice(kv * AW // KVH, (kv + 1) * AW // KVH)
                        last = V.scalar_tensor_tensor(placed[:, kv], ps_z[0][:, cols].rearrange("p (h d) -> p h d", d=HD),
                                                      rstd[:], bias[:, cols].rearrange("p (h d) -> p h d", d=HD),
                                                      ALU.mult, ALU.add)
                    last.then_inc(v_z, 1)
                    return
                V.scalar_tensor_tensor(z[:, a:b], ps_z[c % 2][:, 0:b - a], rstd[:], bias[:, a:b],
                                       ALU.mult, ALU.add).then_inc(v_z, 1)

            def rope_qk(i):
                heads = z[:, 0:AW + KVW].rearrange("p (h d) -> p h d", d=HD)
                both = (P, HEADS + KVH, ROT)
                half = (P, HEADS + KVH, ROT // 2)
                table = rope_sb[:, bass.ds(i, 1), :, :].rearrange("p t a c -> p (t a) c")
                V.drain()
                V.tensor_tensor(rot1[:], heads[:, :, 0:ROT], table[:, 0:1, :].to_broadcast(both), ALU.mult)
                V.tensor_tensor(rot2[:, :, 0:ROT // 2], heads[:, :, ROT // 2:ROT],
                                table[:, 1:2, 0:ROT // 2].to_broadcast(half), ALU.mult)
                V.tensor_tensor(rot2[:, :, ROT // 2:ROT], heads[:, :, 0:ROT // 2],
                                table[:, 1:2, ROT // 2:ROT].to_broadcast(half), ALU.mult)
                V.drain()
                V.tensor_tensor(heads[:, :, 0:ROT], rot1[:], rot2[:], ALU.add).then_inc(v_rope, 1)

            def step(i, a, b, nx, first, second):
                m = i - 1
                vv = uv[:, GW:2 * GW].rearrange("p (g c) -> p g c", c=GC)
                per_group = (P, GG, GC)
                if b:
                    dve.wait_ge(a_gsq, m + 1)
                    V.tensor_scalar(gel[:], gel[:], 0.044715, 1.0, ALU.mult, ALU.add)
                    V.drain()
                    V.tensor_tensor(gel[:], gel[:], z[:, G0:DIN], ALU.mult).then_inc(v_gp, 1)
                if a:
                    dve.wait_ge(p_rstd, i + 1)
                    z_chunk(i, 0)
                if b:
                    dve.wait_ge(a_tanh, m + 1)
                    V.scalar_tensor_tensor(uv[:], gel[:], 1.0, z[:, G0:DIN], ALU.add, ALU.mult)
                    V.drain()
                    V.reduce_sum(st8[:], vv, axis=X)
                    V.drain()
                    V.tensor_scalar(mean8[:], st8[:], 1.0 / GC, None, ALU.mult)
                    V.drain()
                    V.tensor_tensor(vv, vv, mean8[:].unsqueeze(2).to_broadcast(per_group), ALU.subtract).then_inc(v_cen, 1)
                    dve.wait_ge(pe_s, m + 1)
                    V.reduce_max(mx[:], ps_s[:], axis=X)
                    V.drain()
                    V.tensor_tensor(mx[:], mx[:], sink[:], ALU.max)
                    V.drain()
                    V.tensor_scalar(neg_mx[:], mx[:], -1.0, None, ALU.mult)
                    V.tensor_tensor(sink_d[:], sink[:], mx[:], ALU.subtract).then_inc(v_max, 1)
                    dve.wait_ge(a_vsq, m + 1)
                    V.reduce_sum(var8[:], vsq[:].rearrange("p (g c) -> p g c", c=GC), axis=X).then_inc(v_var, 1)
                    dve.wait_ge(p_var, m + 1)
                    V.tensor_tensor(vv, vv, var8[:].unsqueeze(2).to_broadcast(per_group), ALU.mult).then_inc(v_vn, 1)
                if a:
                    z_chunk(i, 1)
                    rope_qk(i)
                    z_chunk(i, 2)
                if nx:
                    split_x(i + 1, False)
                if a:
                    z_chunk(i, 3)
                if b:
                    dve.wait_ge(pe_pv, m + 1)
                    dve.wait_ge(a_exp, m + 1)
                    if not second:
                        dve.wait_ge(st_mix, 16 * m)
                    o = ps_o[:, :, 0:GRP * (HD + 1)].rearrange("p k (h d) -> p k h d", d=HD + 1)
                    den3 = den[:].rearrange("p (k h) -> p k h", k=KVH)
                    V.tensor_tensor(den3, o[:, :, :, HD], sink_e[:].rearrange("p (k h) -> p k h", k=KVH), ALU.add)
                    V.drain()
                    V.reciprocal(den[:], den[:])
                    V.drain()
                    for kv in range(KVH):
                        V.tensor_tensor(mix[:, kv * 256:(kv + 1) * 256].rearrange("p (h d) -> p h d", d=HD),
                                        o[:, kv, :, 0:HD],
                                        den3[:, kv, :].unsqueeze(2).to_broadcast((P, GRP, HD)), ALU.mult)
                    dve.wait_ge(pe_sg, m + 1)
                    mo = mix[:, AW:D]
                    V.tensor_tensor(mo, ps_s[:, 0:GRP, :].rearrange("p a b -> p (a b)"), lng[:], ALU.mult)
                    V.drain()
                    V.tensor_tensor(mo, mo, gate_bias[:], ALU.add)
                    V.drain()
                    V.scalar_tensor_tensor(mo, uv[:, 0:GW], 0.5, mo, ALU.mult, ALU.mult).then_inc(v_o, 1)
                if a:
                    dve.wait_ge(pe_qk, i + 1)
                    if first:
                        V.tensor_copy(kT_mix[:, CHUNK:P], ps_t[:, GRP, 0:CHUNK])
                    else:
                        V.tensor_copy(kT_mix[:, CHUNK:P], kT_cur[:, CHUNK:P])
                    V.tensor_copy(kT_mix[:, 0:CHUNK], ps_t[:, GRP, 0:CHUNK])
                    V.drain()
                    V.tensor_copy(kT_cur[:], ps_t[:, GRP, :]).then_inc(v_kt, 1)
                    zv = z[:, V0:G0].rearrange("p (k d) -> p k d", d=HD)
                    if not first:
                        V.tensor_copy(v_mix[CHUNK:P], v_cur[CHUNK:P])
                    V.tensor_copy(v_mix[0:CHUNK, :, 0:HD], zv[0:CHUNK])
                    V.drain()
                    V.tensor_copy(v_cur[:, :, 0:HD], zv).then_inc(v_vv, 1)

            V.memset(v_cur[:], 1.0)
            V.memset(v_mix[0:CHUNK], 1.0)
            V.memset(v_mix[CHUNK:P], 0.0)
            dve.wait_ge(ld_small, 16 * N_SMALL)
            dve.wait_ge(pe_wsT, 1)
            V.tensor_copy(wsT[:], ps_s[:])
            V.drain()
            V.memset(wsT[CHUNK:P, :, 0:CHUNK], 0.0)
            V.drain().then_inc(v_wsT, 1)
            dve.wait_ge(pe_gb, 1)
            V.tensor_tensor(gate_bias[:].rearrange("p (g c) -> p g c", c=GC),
                            ps_s[:, 0:GRP, :].rearrange("p a (b c) -> p (a b) c", c=GC),
                            bs_sb[:].unsqueeze(2).to_broadcast((P, GG, GC)), ALU.add).then_inc(v_init, 1)
            for k in range(KT):
                dve.wait_ge(a_whi, k + 1)
                V.scalar_tensor_tensor(w_lo[:, k, :], w_raw[k % 2][:], gmix[:, k:k + 1], w_hi[:, k, :].bitcast(F32),
                                       ALU.mult, ALU.subtract).then_inc(v_wlo, 1)
            split_x(0, True)
            step(0, True, False, True, True, False)
            step(1, True, True, True, False, True)
            with dve.Fori(2, NT - 1) as i:
                step(i, True, True, True, False, False)
            step(NT - 1, True, True, False, False, False)
            step(NT, False, True, False, False, False)

        @block.gpsimd
        def _(pool):
            def inverse_root(out, sums, n, eps=EPS):
                nc.gpsimd.tensor_scalar(out, sums, 1.0 / n, eps, ALU.mult, ALU.add)
                nc.gpsimd.drain()
                return nc.gpsimd.tensor_tensor(out, out, minus_half[:, 0:out.shape[1]], ALU.pow)

            def step(i, a, b, first):
                if a:
                    if not first:
                        pool.wait_ge(v_z, 4 * i)
                    pool.wait_ge(a_ssq, i + 1)
                    pool.sem_inc(p_held, 1)
                    inverse_root(rstd[:], ssq[:], D).then_inc(p_rstd, 1)
                if b:
                    pool.wait_ge(v_var, i)
                    pool.sem_inc(p_held, 1)
                    inverse_root(var8[:], var8[:], GC, 4 * EPS).then_inc(p_var, 1)
                    pool.wait_ge(a_nsq, i)
                    pool.sem_inc(p_held, 1)
                    inverse_root(nrs[:], nss[:], AW).then_inc(p_nrs, 1)

            nc.gpsimd.memset(minus_half[:], -0.5)
            nc.gpsimd.drain()
            step(0, True, False, True)
            step(1, True, True, False)
            with pool.Fori(2, NT) as i:
                step(i, True, True, False)
            step(NT, False, True, False)


def after(engine, semaphore, count):
    if not isinstance(count, int) or count > 0:
        engine.wait_ge(semaphore, count)


def within(i, low, high):
    return not isinstance(i, int) or low <= i <= high


def project(nc, x, mix_dram, w_out, g_attn, g_gmlp, g_ffn, w_rg, b_rg, w_re, b_re, mats, toks, pad,
            h_dram, hn_dram, table, bstart, brow):
    NR = NG + NE
    NEG = -3.0e38
    with ExitStack() as ctx:
        sb, pb, sem = makers(ctx, nc, "project")

        wo_hi = sb("wo_hi", [P, KT, D], F32R)
        wo_lo = sb("wo_lo", [P, KT, D], BF16)
        wo_raw = [sb(f"wo_raw{s}", [P, D]) for s in range(2)]
        gains = sb("gains", [P, KT])
        gffn = sb("gffn", [P, D])
        mats_sb = sb("mats_sb", [P, 3 * P + NE])
        ident = mats_sb[:, 0:P]
        iota = mats_sb[:, 3 * P:3 * P + NE]
        before = sb("before", [P, P], BF16)
        ones = sb("ones", [P, P], BF16)
        toks_sb = sb("toks_sb", [P, NT], I32)
        w_r = sb("w_r", [P, KT, NR])
        b_r = sb("b_r", [P, NR])
        zero = sb("zero", [P, D])
        mixt = sb("mixt", [P, D])
        mT_hi = sb("mT_hi", [P, KT, P], F32R)
        mT_lo = sb("mT_lo", [P, KT, P], F32R)
        mT_b = sb("mT_b", [P, KT, P], BF16)
        xt = sb("xt", [P, D])
        h = sb("h", [P, D])
        hn = sb("hn", [P, D])
        hnT = sb("hnT", [P, KT, P])
        junk = sb("junk", [P, D])
        ssq = sb("ssq", [P, 1])
        rstd = sb("rstd", [P, 1])
        minus_half = sb("minus_half", [P, 1])
        lg = sb("lg", [P, 8])
        le = sb("le", [P, NE])
        gtop = sb("gtop", [P, 8])
        gidx = sb("gidx", [P, 8], U32)
        gidx_f = sb("gidx_f", [P, 1])
        gbase = sb("gbase", [P, 1])
        neg_g = sb("neg_g", [P, 1])
        goh = sb("goh", [P, NG])
        lsel = sb("lsel", [P, NG, EPG])
        esel = sb("esel", [P, EPG])
        etop = sb("etop", [P, 8])
        eidx = sb("eidx", [P, 8], U32)
        neg_e = sb("neg_e", [P, 1])
        eid = sb("eid", [P, 2])
        oh = sb("oh", [P, 2, NE])
        oh_sum = sb("oh_sum", [P, NE], BF16)
        oh_acc = sb("oh_acc", [P, NE], BF16)
        gjunk = sb("gjunk", [P, NG])
        gsum = sb("gsum", [P, 1])
        ed = sb("ed", [P, 1])
        wden = sb("wden", [P, 1])
        wts = sb("wts", [P, 2])
        rk = sb("rk", [P, 2, NE])
        rank = sb("rank", [P, 2])
        dest_f = sb("dest_f", [P, 2])
        dest = sb("dest", [P, 2], I32)
        entry = sb("entry", [P, 2, ENTRY], I32)
        cnt_i = sb("cnt_i", [P, NE], I32)
        blocks = sb("blocks", [1, NE])
        ended = sb("ended", [1, MAXB, NE])
        iota_b = sb("iota_b", [1, MAXB])
        owner = sb("owner", [1, MAXB])
        gone = sb("gone", [1, MAXB])
        scan = [sb(f"scan{s}", [P, NE]) for s in range(2)]

        ps_t = pb("ps_t", [P, KT, P])
        ps_y = pb("ps_y", [P, D])
        ps_h = pb("ps_h", [P, KT, P])
        ps_r = pb("ps_r", [P, 512])
        ps_k = pb("ps_k", [P, 512])

        ld_w = [sem(f"ld_wo{s}") for s in range(2)]
        ld_small = sem("ld_small")
        ld_mix = sem("ld_mix")
        ld_x = sem("ld_x")
        st_h = sem("st_h")
        st_hn = sem("st_hn")
        st_pad = sem("st_pad")
        st_ent = sem("st_ent")
        a_whi = sem("a_whi")
        v_wlo = sem("v_wlo")
        v_init = sem("v_init")
        pe_mt = sem("pe_mt")
        pe_y = sem("pe_y")
        pe_ht = sem("pe_ht")
        pe_r = sem("pe_r")
        pe_rk = sem("pe_rk")
        a_mh = sem("a_mh")
        a_hsq = sem("a_hsq")
        a_ht = sem("a_ht")
        a_ex = sem("a_ex")
        p_rstd = sem("p_rstd")
        p_held = sem("p_held")
        v_ml = sem("v_ml")
        v_h = sem("v_h")
        v_hn = sem("v_hn")
        v_g = sem("v_g")
        v_oh = sem("v_oh")
        v_ent = sem("v_ent")
        v_acc = sem("v_acc")

        x_t = x.rearrange("b (t p) d -> (b t) p d", p=P)
        mix_t = mix_dram.rearrange("(t p) d -> t p d", p=P)
        h_t = h_dram.rearrange("(t p) d -> t p d", p=P)
        hn_t = hn_dram.rearrange("(t p) d -> t p d", p=P)
        wo_t = w_out.rearrange("l (k p) n -> (l k) p n", p=P)
        N_SMALL = 10
        HALF = KT // 2

        block = ctx.enter_context(nc.Block())
        STEADY = (4, NT - 2)
        STEPS = NT + 3

        def all_steps(engine, step):
            for i in range(STEADY[0]):
                step(i)
            with engine.Fori(*STEADY) as i:
                step(i)
            for i in range(STEADY[1], STEPS):
                step(i)

        @block.sync
        def _(sp):
            def load_mix(n):
                after(sp, pe_mt, n)
                sp.dma_start(mixt[:], mix_t[bass.ds(n, 1)].rearrange("a p d -> (a p) d")).then_inc(ld_mix, 16)

            def load_x(n):
                after(sp, v_h, n)
                sp.dma_start(xt[:], x_t[bass.ds(n, 1)].rearrange("a p d -> (a p) d")).then_inc(ld_x, 16)

            def step(i):
                if within(i, 0, NT - 3):
                    load_mix(i + 2)
                if within(i, 1, NT):
                    m = i - 1
                    sp.wait_ge(v_h, m + 1)
                    sp.dma_start(h_t[bass.ds(m, 1)].rearrange("a p d -> (a p) d"), h[:]).then_inc(st_h, 16)
                    if within(i, 1, NT - 1):
                        load_x(i)
                    sp.wait_ge(v_hn, m + 1)
                    sp.dma_start(hn_t[bass.ds(m, 1)].rearrange("a p d -> (a p) d"), hn[:]).then_inc(st_hn, 16)

            sp.dma_start(mats_sb[:], mats[:, 0:3 * P + NE]).then_inc(ld_small, 16)
            sp.dma_start(iota_b[:], mats[0:1, 3 * P:3 * P + MAXB]).then_inc(ld_small, 16)
            for n, g in enumerate((g_attn, g_gmlp)):
                sp.dma_start(gains[:, n * HALF:(n + 1) * HALF], g.rearrange("l (k p) -> p (l k)", p=P),
                             allow_slow_non_contiguous=True).then_inc(ld_small, 16)
            load_mix(0)
            load_x(0)
            for k in range(KT):
                after(sp, v_wlo, k - 1)
                sp.dma_start(wo_raw[k % 2][:], wo_t[k]).then_inc(ld_w[k % 2], 16)
                if k == 1:
                    sp.dma_start(toks_sb[:], toks).then_inc(ld_small, 16)
                    sp.dma_start(w_r[:, :, 0:NG], w_rg.rearrange("l (k p) n -> p (l k) n", p=P)).then_inc(ld_small, 16)
                    sp.dma_start(w_r[:, :, NG:NR], w_re.rearrange("l (k p) n -> p (l k) n", p=P)).then_inc(ld_small, 16)
                    sp.dma_start(b_r[:, 0:NG], b_rg.to_broadcast((P, NG))).then_inc(ld_small, 16)
                    sp.dma_start(b_r[:, NG:NR], b_re.to_broadcast((P, NE))).then_inc(ld_small, 16)
                    sp.dma_start(gffn[:], g_ffn.to_broadcast((P, D))).then_inc(ld_small, 16)
                    sp.dma_start(table.rearrange("(p j) c -> p (j c)", p=P),
                                 pad.rearrange("(p j) c -> p (j c)", p=P)).then_inc(st_pad, 16)
            load_mix(1)
            sp.wait_ge(v_init, 1)
            sp.dma_start(h_t[NT], zero[:]).then_inc(st_pad, 16)
            all_steps(sp, step)
            sp.wait_ge(st_h, 16 * NT)
            sp.wait_ge(st_hn, 16 * NT)
            sp.wait_ge(st_pad, 32)

        @block.tensor
        def _(pe):
            def mix_transposes(n):
                pe.wait_ge(ld_mix, 16 * (n + 1))
                after(pe, v_ml, 2 * n)
                for k in range(KT):
                    last = nc.tensor.transpose(ps_t[:, k, :], mixt[:, k * P:(k + 1) * P], ident)
                last.then_inc(pe_mt, 1)

            def half_product(i, half):
                pe.wait_ge(v_ml, 2 * i + half + 1)
                for k in range(half * HALF, (half + 1) * HALF):
                    for c in range(2):
                        out, cols = ps_y[:, c * 512:(c + 1) * 512], slice(c * 512, (c + 1) * 512)
                        nc.tensor.matmul(out, mT_hi[:, k, :], wo_hi[:, k, cols], start=(k == 0), stop=False)
                        nc.tensor.matmul(out, mT_lo[:, k, :], wo_hi[:, k, cols], start=False, stop=False)
                        last = nc.tensor.matmul(out, mT_b[:, k, :], wo_lo[:, k, cols], start=False, stop=(k == KT - 1))
                last.then_inc(pe_y, 1)

            def step(i):
                m, r = i - 1, i - 2
                if within(i, 0, NT - 2):
                    mix_transposes(i + 1)
                if within(i, 0, NT - 1):
                    after(pe, v_h, i)
                    half_product(i, 0)
                if within(i, 1, NT):
                    pe.wait_ge(v_hn, m + 1)
                    after(pe, a_ht, m)
                    for k in range(KT):
                        last = nc.tensor.transpose(ps_h[:, k, :], hn[:, k * P:(k + 1) * P], ident)
                    last.then_inc(pe_ht, 1)
                if within(i, 0, NT - 1):
                    half_product(i, 1)
                if within(i, 1, NT):
                    pe.wait_ge(a_ht, m + 1)
                    after(pe, v_oh, m)
                    for k in range(KT):
                        last = nc.tensor.matmul(ps_r[:, 0:NR], hnT[:, k, :], w_r[:, k, :], start=(k == 0), stop=(k == KT - 1))
                    last.then_inc(pe_r, 1)
                if within(i, 2, NT + 1):
                    pe.wait_ge(v_oh, r + 1)
                    after(pe, v_ent, r)
                    nc.tensor.matmul(ps_k[:, 0:NE], before[:], oh_sum[:], start=True, stop=False)
                    nc.tensor.matmul(ps_k[:, 0:NE], ones[:], oh_acc[:], start=False, stop=True).then_inc(pe_rk, 1)

            pe.wait_ge(ld_small, 16 * N_SMALL)
            mix_transposes(0)
            pe.wait_ge(v_init, 1)
            pe.wait_ge(v_wlo, KT)
            all_steps(pe, step)
            pe.wait_ge(v_acc, 1)
            nc.tensor.matmul(ps_k[:, 0:NE], ones[:], oh_acc[:], start=True, stop=True).then_inc(pe_rk, 1)

        @block.scalar
        def _(act):
            def split_half(n, half):
                act.wait_ge(pe_mt, n + 1)
                after(act, pe_y, 2 * n - 1 + half)
                ks = slice(half * HALF, (half + 1) * HALF)
                nc.scalar.copy(mT_hi[:, ks, :], ps_t[:, ks, :]).then_inc(a_mh, 1)

            def step(i):
                m, r = i - 1, i - 2
                if within(i, 1, NT):
                    act.wait_ge(v_h, m + 1)
                    after(act, p_rstd, m)
                    nc.scalar.activation(junk[:], h[:], ACT.Square, accum_out=ssq[:]).then_inc(a_hsq, 1)
                if within(i, 0, NT - 2):
                    split_half(i + 1, 0)
                if within(i, 1, NT):
                    act.wait_ge(pe_ht, m + 1)
                    after(act, pe_r, m)
                    nc.scalar.copy(hnT[:], ps_h[:]).then_inc(a_ht, 1)
                if within(i, 2, NT + 1):
                    act.wait_ge(v_g, r + 1)
                    nc.scalar.activation(gjunk[:], lg[:, 0:NG], ACT.Exp, bias=neg_g[:], accum_out=gsum[:])
                    nc.scalar.activation(ed[:], etop[:, 1:2], ACT.Exp, bias=neg_e[:]).then_inc(a_ex, 1)
                if within(i, 0, NT - 2):
                    split_half(i + 1, 1)

            act.wait_ge(ld_small, 16 * N_SMALL)
            for k in range(KT):
                act.wait_ge(ld_w[k % 2], 16 * (k // 2 + 1))
                nc.scalar.mul(wo_hi[:, k, :], wo_raw[k % 2][:], gains[:, k:k + 1]).then_inc(a_whi, 1)
            split_half(0, 0)
            split_half(0, 1)
            all_steps(act, step)

        @block.vector
        def _(dve):
            V = nc.vector

            def split_half(n, half):
                dve.wait_ge(a_mh, 2 * n + half + 1)
                after(dve, pe_y, 2 * n - 1 + half)
                ks = slice(half * HALF, (half + 1) * HALF)
                V.tensor_copy(mT_b[:, ks, :], mT_hi[:, ks, :].bitcast(F32))
                V.tensor_tensor(mT_lo[:, ks, :], ps_t[:, ks, :], mT_hi[:, ks, :].bitcast(F32), ALU.subtract).then_inc(v_ml, 1)

            def entries(s):
                dve.wait_ge(pe_rk, s + 1)
                V.tensor_tensor(rk[:], oh[:], ps_k[:, 0:NE].unsqueeze(1).to_broadcast((P, 2, NE)), ALU.mult)
                V.tensor_tensor(oh_acc[:], oh_acc[:], oh_sum[:], ALU.add)
                V.drain()
                V.reduce_sum(rank[:], rk[:], axis=X)
                V.drain()
                V.scalar_tensor_tensor(dest_f[:], eid[:], float(ROWS_PER_EXPERT), rank[:], ALU.mult, ALU.add)
                after(dve, st_ent, 32 * s)
                for k in range(2):
                    for c in range(2):
                        V.tensor_copy(entry[:, k, c:c + 1], toks_sb[:, bass.ds(s, 1)])
                V.tensor_copy(entry[:, :, 2].bitcast(F32), wts[:])
                V.drain()
                V.tensor_copy(dest[:], dest_f[:]).then_inc(v_ent, 1)

            def route(r):
                dve.wait_ge(pe_r, r + 1)
                V.tensor_tensor(lg[:, 0:NG], ps_r[:, 0:NG], b_r[:, 0:NG], ALU.add)
                V.tensor_tensor(le[:], ps_r[:, NG:NR], b_r[:, NG:NR], ALU.add)
                V.drain()
                V.max(gtop[:], lg[:])
                V.drain()
                V.max_index(gidx[:], gtop[:], lg[:])
                V.tensor_scalar(neg_g[:], gtop[:, 0:1], -1.0, None, ALU.mult)
                V.drain()
                V.tensor_copy(gidx_f[:], gidx[:, 0:1])
                V.drain()
                V.tensor_scalar(goh[:], iota[:, 0:NG], gidx_f[:], None, ALU.is_equal)
                V.tensor_scalar(gbase[:], gidx_f[:], float(EPG), None, ALU.mult)
                V.drain()
                V.tensor_tensor(lsel[:], le[:].rearrange("p (g e) -> p g e", g=NG),
                                goh[:].unsqueeze(2).to_broadcast((P, NG, EPG)), ALU.mult)
                V.drain()
                V.reduce_sum(esel[:], lsel[:].rearrange("p g e -> p e g"), axis=X)
                V.drain()
                V.max(etop[:], esel[:])
                V.drain()
                V.max_index(eidx[:], etop[:], esel[:])
                V.tensor_scalar(neg_e[:], etop[:, 0:1], -1.0, None, ALU.mult).then_inc(v_g, 1)
                V.drain()
                V.tensor_copy(eid[:], eidx[:, 0:2])
                V.drain()
                V.tensor_scalar(eid[:], eid[:], gbase[:], None, ALU.add)
                V.drain()
                V.tensor_tensor(oh[:], iota.unsqueeze(1).to_broadcast((P, 2, NE)),
                                eid[:].unsqueeze(2).to_broadcast((P, 2, NE)), ALU.is_equal)
                V.drain()
                V.tensor_tensor(oh_sum[:], oh[:, 0, :], oh[:, 1, :], ALU.add).then_inc(v_oh, 1)
                dve.wait_ge(a_ex, r + 1)
                V.tensor_scalar(wden[:], ed[:], 1.0, gsum[:], ALU.add, ALU.mult)
                V.drain()
                V.reciprocal(wts[:, 0:1], wden[:])
                V.drain()
                V.tensor_tensor(wts[:, 1:2], wts[:, 0:1], ed[:], ALU.mult)
                V.drain()

            def step(i):
                m, r, s = i - 1, i - 2, i - 3
                if within(i, 1, NT):
                    dve.wait_ge(pe_y, 2 * m + 2)
                    dve.wait_ge(ld_x, 16 * (m + 1))
                    after(dve, st_h, 16 * m)
                    V.tensor_tensor(h[:], ps_y[:], xt[:], ALU.add).then_inc(v_h, 1)
                if within(i, 3, NT + 2):
                    entries(s)
                if within(i, 1, NT):
                    dve.wait_ge(p_rstd, m + 1)
                    after(dve, st_hn, 16 * m)
                    after(dve, pe_ht, m)
                    V.scalar_tensor_tensor(hn[:], h[:], rstd[:], gffn[:], ALU.mult, ALU.mult).then_inc(v_hn, 1)
                if within(i, 0, NT - 2):
                    split_half(i + 1, 0)
                if within(i, 2, NT + 1):
                    route(r)
                if within(i, 0, NT - 2):
                    split_half(i + 1, 1)

            V.memset(zero[:], 0.0)
            V.memset(lg[:], NEG)
            V.memset(oh_acc[:], 0.0)
            V.memset(entry[:], 0)
            dve.wait_ge(ld_small, 16 * N_SMALL)
            V.tensor_copy(before[:], mats_sb[:, P:2 * P])
            V.tensor_copy(ones[:], mats_sb[:, 2 * P:3 * P])
            V.drain().then_inc(v_init, 1)
            for k in range(KT):
                dve.wait_ge(a_whi, k + 1)
                V.scalar_tensor_tensor(wo_lo[:, k, :], wo_raw[k % 2][:], gains[:, k:k + 1], wo_hi[:, k, :].bitcast(F32),
                                       ALU.mult, ALU.subtract).then_inc(v_wlo, 1)
            split_half(0, 0)
            split_half(0, 1)
            all_steps(dve, step)
            V.drain().then_inc(v_acc, 1)
            dve.wait_ge(pe_rk, NT + 1)
            V.tensor_scalar(scan[0][:], ps_k[:, 0:NE], float(BLK - 1), None, ALU.add)
            V.drain()
            V.tensor_copy(cnt_i[:], scan[0][:])
            V.drain()
            V.tensor_scalar(cnt_i[:], cnt_i[:], 7, None, ALU.arith_shift_right)
            V.drain()
            V.tensor_copy(scan[0][:], cnt_i[:])
            V.drain()
            V.tensor_scalar(scan[0][:], scan[0][:], 2.0, None, ALU.max)
            V.drain()
            V.tensor_copy(blocks[:], scan[0][0:1, :])
            s, d = 0, 1
            while d < NE:
                V.tensor_copy(scan[1 - s][:, 0:d], scan[s][:, 0:d])
                V.tensor_tensor(scan[1 - s][:, d:NE], scan[s][:, d:NE], scan[s][:, 0:NE - d], ALU.add)
                V.drain()
                s, d = 1 - s, 2 * d
            V.memset(bstart[:], 0)
            V.drain()
            V.tensor_copy(bstart[0:1, 1:NE + 1], scan[s][0:1, :])
            grid = (1, MAXB, NE)
            V.tensor_tensor(ended[:], scan[s][0:1, :].unsqueeze(1).to_broadcast(grid),
                            iota_b[:].unsqueeze(2).to_broadcast(grid), ALU.is_le)
            V.drain()
            V.reduce_sum(owner[:], ended[:], axis=X)
            V.drain()
            V.tensor_tensor(ended[:], ended[:], blocks[:].unsqueeze(1).to_broadcast(grid), ALU.mult)
            V.drain()
            V.reduce_sum(gone[:], ended[:], axis=X)
            V.drain()
            V.tensor_tensor(gone[:], iota_b[:], gone[:], ALU.subtract)
            V.tensor_scalar(owner[:], owner[:], float(ROWS_PER_EXPERT), None, ALU.mult)
            V.drain()
            V.scalar_tensor_tensor(owner[:], gone[:], float(BLK), owner[:], ALU.mult, ALU.add)
            V.drain()
            V.tensor_scalar(brow[:], owner[:], float(NE * ROWS_PER_EXPERT - BLK), None, ALU.min)

        @block.gpsimd
        def _(pool):
            def step(i):
                m, s = i - 1, i - 3
                if within(i, 1, NT):
                    pool.wait_ge(a_hsq, m + 1)
                    after(pool, v_hn, m)
                    pool.sem_inc(p_held, 1)
                    nc.gpsimd.tensor_scalar(rstd[:], ssq[:], 1.0 / D, EPS, ALU.mult, ALU.add)
                    nc.gpsimd.drain()
                    nc.gpsimd.tensor_tensor(rstd[:], rstd[:], minus_half[:], ALU.pow).then_inc(p_rstd, 1)
                if within(i, 3, NT + 2):
                    pool.wait_ge(v_ent, s + 1)
                    pool.sem_inc(p_held, 1)
                    for k in range(2):
                        nc.gpsimd.indirect_dma_start(
                            out=table, out_offset=bass.IndirectOffsetOnAxis(ap=dest[:, k:k + 1], axis=0),
                            in_=entry[:, k, :], in_offset=None).then_inc(st_ent, 16)

            nc.gpsimd.memset(minus_half[:], -0.5)
            nc.gpsimd.drain()
            pool.wait_ge(st_pad, 32)
            all_steps(pool, step)
            pool.wait_ge(st_ent, 32 * NT)


def experts(nc, w_gate, w_up, w_down, mats, hn_dram, h_dram, table, bstart, brow):
    with ExitStack() as ctx:
        sb, pb, sem = makers(ctx, nc, "experts")

        CH, CW = 6, 2048
        RAW = 3
        RING = 4
        we_hi = [sb(f"we_hi{p}", [P, CH, CW], F32R) for p in range(2)]
        we_lo = [sb(f"we_lo{p}", [P, CH, CW], BF16) for p in range(2)]
        raw = [sb(f"we_raw{s}", [P, CW]) for s in range(RAW)]
        ident = sb("ident", [P, P])
        ring = sb("ring", [P, RING, ENTRY], I32)
        row_in = sb("row_in", [P, ENTRY], I32)
        row_out = sb("row_out", [P, ENTRY], I32)
        xg = sb("xg", [P, D])
        xT_hi = sb("xT_hi", [P, KT, P], F32R)
        xT_lo = sb("xT_lo", [P, KT, P], F32R)
        xT_b = sb("xT_b", [P, KT, P], BF16)
        silu = sb("silu", [P, F])
        hid = sb("hid", [P, F])
        hT_hi = sb("hT_hi", [P, FT, P], F32R)
        hT_lo = sb("hT_lo", [P, FT, P], F32R)
        hT_b = sb("hT_b", [P, FT, P], BF16)
        y = sb("y", [P, D])

        ps_x = pb("ps_x", [P, KT, P])
        ps_g = pb("ps_g", [P, F])
        ps_u = pb("ps_u", [P, F])
        ps_h = pb("ps_h", [P, FT, P])
        ps_y = pb("ps_y", [P, D])

        ld_id = sem("ld_id")
        ld_raw = [sem(f"ld_raw{s}") for s in range(RAW)]
        ld_ring = sem("ld_ring")
        p_in = sem("p_in")
        p_out = sem("p_out")
        ld_x = sem("ld_x")
        st_y = sem("st_y")
        a_w = sem("a_w")
        v_w = sem("v_w")
        pe_xt = sem("pe_xt")
        pe_g = sem("pe_g")
        pe_u = sem("pe_u")
        pe_ht = sem("pe_ht")
        pe_dn = sem("pe_dn")
        a_sl = sem("a_sl")
        a_xh = sem("a_xh")
        a_hh = sem("a_hh")
        a_y = sem("a_y")
        v_hm = sem("v_hm")
        v_xl = sem("v_xl")
        v_hl = sem("v_hl")
        p_y = sem("p_y")
        held = {e: sem(f"held_{e}") for e in ("pe", "act", "pool")}

        block = ctx.enter_context(nc.Block())

        def bounds(engine, e):
            col = bass.ds(e, 1) if not isinstance(e, int) else slice(e, e + 1)
            nxt = bass.ds(e + 1, 1) if not isinstance(e, int) else slice(e + 1, e + 2)
            return (engine.value_load(bstart[0:1, col], min_val=0, max_val=MAXB - 4),
                    engine.value_load(bstart[0:1, nxt], min_val=2, max_val=MAXB - 2))

        def all_experts(engine, expert):
            expert(0, 0, True)
            expert(1, 1, True)
            with engine.Fori(1, NE // 2 - 1) as pair:
                expert(2 * pair, 0, True)
                expert(2 * pair + 1, 1, True)
            expert(NE - 2, 0, True)
            expert(NE - 1, 1, False)

        def source(c, e):
            if c < 4:
                w = (w_gate, w_up)[c // 2].rearrange("l e (k p) n -> (l e) p k n", p=P)
                part = slice((c % 2) * KT // 2, (c % 2 + 1) * KT // 2)
            else:
                w = w_down.rearrange("l e (k p) n -> (l e) p k n", p=P)
                part = slice((c % 2) * FT // 2, (c % 2 + 1) * FT // 2)
            return w[bass.ds(e, 1), :, part, :].rearrange("a p k n -> (a p) k n")

        @block.sync
        def _(sp):
            sp.dma_start(ident[:], mats[:, 0:P]).then_inc(ld_id, 16)

            def load_weights(e):
                for c in range(CH):
                    after(sp, v_w, CH * e + c + 1 - RAW)
                    width = F if c < 4 else D
                    sp.dma_start(raw[c % RAW][:].rearrange("p (k n) -> p k n", n=width),
                                 source(c, e)).then_inc(ld_raw[c % RAW], 16)

            load_weights(0)
            with sp.Fori(1, NE) as e:
                load_weights(e)

        @block.tensor
        def _(pe):
            def x_transposes(n):
                pe.wait_ge(ld_x, 16 * (n + 1))
                for k in range(KT):
                    last = nc.tensor.transpose(ps_x[:, k, :], xg[:, k * P:(k + 1) * P], ident[:])
                last.then_inc(pe_xt, 1)

            def project_in(out, first_chunk, p):
                for k in range(KT):
                    cols = slice((k % 4) * F, (k % 4 + 1) * F)
                    c = first_chunk + k // 4
                    nc.tensor.matmul(out, xT_hi[:, k, :], we_hi[p][:, c, cols], start=(k == 0), stop=False)
                    nc.tensor.matmul(out, xT_lo[:, k, :], we_hi[p][:, c, cols], start=False, stop=False)
                    last = nc.tensor.matmul(out, xT_b[:, k, :], we_lo[p][:, c, cols], start=False, stop=(k == KT - 1))
                return last

            def down(g, p):
                pe.wait_ge(a_y, g + 1)
                pe.wait_ge(v_hl, g + 1)
                for half in range(2):
                    out = ps_y[:, half * 512:(half + 1) * 512]
                    for k in range(FT):
                        c, a = 4 + k // 2, (k % 2) * D + half * 512
                        nc.tensor.matmul(out, hT_hi[:, k, :], we_hi[p][:, c, a:a + 512], start=(k == 0), stop=False)
                        nc.tensor.matmul(out, hT_lo[:, k, :], we_hi[p][:, c, a:a + 512], start=False, stop=False)
                        last = nc.tensor.matmul(out, hT_b[:, k, :], we_lo[p][:, c, a:a + 512], start=False, stop=(k == FT - 1))
                last.then_inc(pe_dn, 1)

            def run_block(g, p, down_p):
                pe.wait_ge(v_xl, g + 1)
                project_in(ps_g[:], 0, p).then_inc(pe_g, 1)
                project_in(ps_u[:], 2, p).then_inc(pe_u, 1)
                x_transposes(g + 1)
                if down_p is not None:
                    down(g - 1, down_p)
                pe.wait_ge(v_hm, g + 1)
                for k in range(FT):
                    last = nc.tensor.transpose(ps_h[:, k, :], hid[:, k * P:(k + 1) * P], ident[:])
                last.then_inc(pe_ht, 1)

            def expert(e, p, prefetch):
                g0, g1 = bounds(pe, e)
                pe.wait_ge(v_w, CH * (e + 1))
                run_block(g0, p, None if isinstance(e, int) and e == 0 else 1 - p)
                with pe.Fori(g0 + 1, g1) as g:
                    run_block(g, p, p)

            pe.sem_inc(pe_dn, 1)
            pe.wait_ge(ld_id, 16)
            x_transposes(0)
            all_experts(pe, expert)
            down(pe.value_load(bstart[0:1, NE:NE + 1], min_val=2, max_val=MAXB - 2) - 1, 1)

        @block.scalar
        def _(act):
            def split_weights(e, c, p):
                act.wait_ge(ld_raw[c % RAW], 16 * (2 * e + c // RAW + 1))
                nc.scalar.copy(we_hi[p][:, c, :], raw[c % RAW][:]).then_inc(a_w, 1)

            def split_x(n):
                act.wait_ge(pe_xt, n + 1)
                nc.scalar.copy(xT_hi[:], ps_x[:]).then_inc(a_xh, 1)

            def weigh(g):
                act.wait_ge(pe_dn, g + 2)
                act.wait_ge(p_out, g + 1)
                act.wait_ge(p_y, g + 1)
                act.sem_inc(held["act"], 1)
                nc.scalar.mul(y[:], ps_y[:], row_out[:, 2:3].bitcast(F32)).then_inc(a_y, 1)

            def run_block(g, weights, first=False):
                weights(0)
                weights(1)
                act.wait_ge(pe_g, g + 1)
                nc.scalar.activation(silu[:], ps_g[:], ACT.Silu).then_inc(a_sl, 1)
                weights(2)
                split_x(g + 1)
                weights(3)
                if not first:
                    weigh(g - 1)
                act.wait_ge(pe_ht, g + 1)
                nc.scalar.copy(hT_hi[:], ps_h[:]).then_inc(a_hh, 1)
                weights(4)
                weights(5)

            def expert(e, p, prefetch):
                g0, g1 = bounds(act, e)
                run_block(g0, (lambda c: split_weights(e + 1, c, 1 - p)) if prefetch else (lambda c: None),
                          isinstance(e, int) and e == 0)
                with act.Fori(g0 + 1, g1) as g:
                    run_block(g, lambda c: None)

            act.sem_inc(a_y, 1)
            for c in range(CH):
                split_weights(0, c, 0)
            split_x(0)
            all_experts(act, expert)
            weigh(act.value_load(bstart[0:1, NE:NE + 1], min_val=2, max_val=MAXB - 2) - 1)

        @block.vector
        def _(dve):
            V = nc.vector

            def split_weights(e, c, p):
                dve.wait_ge(a_w, CH * e + c + 1)
                V.tensor_tensor(we_lo[p][:, c, :], raw[c % RAW][:], we_hi[p][:, c, :].bitcast(F32), ALU.subtract).then_inc(v_w, 1)

            def split_x(n):
                dve.wait_ge(a_xh, n + 1)
                V.tensor_copy(xT_b[:], xT_hi[:].bitcast(F32))
                V.tensor_tensor(xT_lo[:], ps_x[:], xT_hi[:].bitcast(F32), ALU.subtract).then_inc(v_xl, 1)

            def run_block(g, weights):
                weights(0)
                weights(1)
                weights(2)
                dve.wait_ge(pe_u, g + 1)
                dve.wait_ge(a_sl, g + 1)
                V.tensor_tensor(hid[:], silu[:], ps_u[:], ALU.mult).then_inc(v_hm, 1)
                split_x(g + 1)
                weights(3)
                dve.wait_ge(a_hh, g + 1)
                V.tensor_copy(hT_b[:], hT_hi[:].bitcast(F32))
                V.tensor_tensor(hT_lo[:], ps_h[:], hT_hi[:].bitcast(F32), ALU.subtract).then_inc(v_hl, 1)
                weights(4)
                weights(5)

            def expert(e, p, prefetch):
                g0, g1 = bounds(dve, e)
                run_block(g0, (lambda c: split_weights(e + 1, c, 1 - p)) if prefetch else (lambda c: None))
                with dve.Fori(g0 + 1, g1) as g:
                    run_block(g, lambda c: None)

            for c in range(CH):
                split_weights(0, c, 0)
            split_x(0)
            all_experts(dve, expert)

        @block.gpsimd
        def _(pool):
            def load_ring(g):
                row = pool.value_load(brow[0:1, bass.ds(g, 1)], min_val=0, max_val=NE * ROWS_PER_EXPERT - BLK)
                pool.dma_start(ring[:, bass.ds(g & (RING - 1), 1), :].rearrange("p a c -> p (a c)"),
                               table[bass.ds(row, BLK), :]).then_inc(ld_ring, 16)

            def gather(g):
                pool.wait_ge(ld_ring, 16 * (g + 1))
                pool.sem_inc(held["pool"], 1)
                nc.gpsimd.tensor_copy(row_in[:], ring[:, bass.ds(g & (RING - 1), 1), :].rearrange("p a c -> p (a c)")).then_inc(p_in, 1)
                pool.wait_ge(p_in, g + 1)
                pool.sem_inc(held["pool"], 1)
                nc.gpsimd.indirect_dma_start(out=xg[:], out_offset=None, in_=hn_dram,
                                             in_offset=bass.IndirectOffsetOnAxis(ap=row_in[:, 0:1], axis=0)).then_inc(ld_x, 16)

            def rows_out(g):
                nc.gpsimd.tensor_copy(row_out[:], ring[:, bass.ds(g & (RING - 1), 1), :].rearrange("p a c -> p (a c)")).then_inc(p_out, 1)

            def add_rows(g):
                pool.wait_ge(a_y, g + 2)
                pool.wait_ge(p_out, g + 1)
                pool.sem_inc(held["pool"], 1)
                nc.gpsimd.indirect_dma_start(out=h_dram, out_offset=bass.IndirectOffsetOnAxis(ap=row_out[:, 1:2], axis=0),
                                             in_=y[:], in_offset=None, compute_op=ALU.add).then_inc(st_y, 16)
                pool.wait_ge(st_y, 16 * (g + 1))
                pool.sem_inc(p_y, 1)

            def step(g, first=False):
                pool.wait_ge(pe_xt, g + 1)
                gather(g + 1)
                load_ring(g + 2)
                if not first:
                    add_rows(g - 1)
                rows_out(g)

            pool.sem_inc(p_y, 1)
            load_ring(0)
            gather(0)
            load_ring(1)
            step(0, True)
            total = pool.value_load(bstart[0:1, NE:NE + 1], min_val=2, max_val=MAXB - 2)
            with pool.Fori(1, total) as g:
                step(g)
            add_rows(total - 1)
            pool.wait_ge(ld_ring, 16 * (total + 2))
            pool.wait_ge(ld_x, 16 * (total + 1))


def final(nc, h_dram, g_final, out):
    SLOTS = 4
    with ExitStack() as ctx:
        sb, pb, sem = makers(ctx, nc, "final")
        gain = sb("gain", [P, D])
        h = [sb(f"hf{s}", [P, D]) for s in range(SLOTS)]
        o = [sb(f"of{s}", [P, D]) for s in range(SLOTS)]
        junk = [sb(f"junk{s}", [P, D]) for s in range(SLOTS)]
        ssq = [sb(f"ssq{s}", [P, 1]) for s in range(SLOTS)]
        rstd = [sb(f"rstd{s}", [P, 1]) for s in range(SLOTS)]
        minus_half = sb("minus_half", [P, 1])
        ld_g = sem("ld_g")
        ld_h = [sem(f"ld_h{s}") for s in range(SLOTS)]
        st_o = [sem(f"st_o{s}") for s in range(SLOTS)]
        a_sq = sem("a_sq")
        p_rs = sem("p_rs")
        p_held = sem("p_held")
        v_o = sem("v_o")
        h_t = h_dram.rearrange("(t p) d -> t p d", p=P)
        out_t = out.rearrange("b (t p) d -> (b t) p d", p=P)
        block = ctx.enter_context(nc.Block())

        def rounds(engine, tile):
            for s in range(SLOTS):
                tile(0, s)
            with engine.Fori(1, NT // SLOTS) as r:
                for s in range(SLOTS):
                    tile(r, s)

        @block.sync
        def _(sp):
            sp.dma_start(gain[:], g_final.rearrange("(a d) -> a d", a=1).to_broadcast((P, D))).then_inc(ld_g, 16)

            def tile(r, s):
                after(sp, v_o, SLOTS * (r - 1) + s + 1)
                sp.dma_start(h[s][:], h_t[bass.ds(SLOTS * r + s, 1)].rearrange("a p d -> (a p) d")).then_inc(ld_h[s], 16)

            rounds(sp, tile)

        @block.scalar
        def _(act):
            def tile(r, s):
                act.wait_ge(ld_h[s], 16 * (r + 1))
                after(act, p_rs, SLOTS * (r - 1) + s + 1)
                nc.scalar.activation(junk[s][:], h[s][:], ACT.Square, accum_out=ssq[s][:]).then_inc(a_sq, 1)
                if not (isinstance(r, int) and s == 0):
                    store(SLOTS * r + s - 1, r if s else r - 1, (s - 1) % SLOTS)

            def store(n, r, s):
                act.wait_ge(v_o, n + 1)
                act.dma_start(out_t[bass.ds(n, 1)].rearrange("a p d -> (a p) d"), o[s][:]).then_inc(st_o[s], 16)

            rounds(act, tile)
            store(NT - 1, NT // SLOTS - 1, SLOTS - 1)
            for s in range(SLOTS):
                act.wait_ge(st_o[s], 16 * (NT // SLOTS))

        @block.gpsimd
        def _(pool):
            nc.gpsimd.memset(minus_half[:], -0.5)
            nc.gpsimd.drain()

            def tile(r, s):
                pool.wait_ge(a_sq, SLOTS * r + s + 1)
                after(pool, v_o, SLOTS * (r - 1) + s + 1)
                pool.sem_inc(p_held, 1)
                nc.gpsimd.tensor_scalar(rstd[s][:], ssq[s][:], 1.0 / D, EPS, ALU.mult, ALU.add)
                nc.gpsimd.drain()
                nc.gpsimd.tensor_tensor(rstd[s][:], rstd[s][:], minus_half[:], ALU.pow).then_inc(p_rs, 1)

            rounds(pool, tile)

        @block.vector
        def _(dve):
            dve.wait_ge(ld_g, 16)

            def tile(r, s):
                dve.wait_ge(p_rs, SLOTS * r + s + 1)
                after(dve, st_o[s], 16 * r)
                nc.vector.scalar_tensor_tensor(o[s][:], h[s][:], rstd[s][:], gain[:], ALU.mult, ALU.mult).then_inc(v_o, 1)

            rounds(dve, tile)


def build(nc, a, out):
    mix_dram = nc.dram_tensor("mix_rows", (SEQ, D), F32, kind="Internal").ap()
    h_dram = nc.dram_tensor("h_rows", (SEQ + P, D), F32, kind="Internal").ap()
    hn_dram = nc.dram_tensor("hn_rows", (SEQ, D), F32, kind="Internal").ap()
    table = nc.dram_tensor("expert_rows", (NE * ROWS_PER_EXPERT, ENTRY), I32, kind="Internal").ap()
    with nc.sbuf_tensor("bstart", [1, NE + 1], I32) as bstart, nc.sbuf_tensor("brow", [1, MAXB], I32) as brow:
        mixers(nc, a["x"], a["w_in"], a["b_in"], a["sinks"], a["gmlp_w_s"], a["gmlp_b_s"], a["gmlp_ln_g"],
               a["gmlp_ln_b"], a["g_mix_norm"], a["mats"], a["rope"], mix_dram)
        project(nc, a["x"], mix_dram, a["w_out"], a["g_attn_out"], a["g_gmlp_out"], a["g_ffn_norm"],
                a["w_router_group"], a["b_router_group"], a["w_router_expert"], a["b_router_expert"],
                a["mats"], a["toks"], a["pad"], h_dram, hn_dram, table, bstart, brow)
        experts(nc, a["w_gate"], a["w_up"], a["w_down"], a["mats"], hn_dram, h_dram, table, bstart, brow)
        final(nc, h_dram, a["g_final"], out)


def shape_constants():
    mats = np.zeros((P, 3 * P + MAXB), np.float32)
    mats[:, 0:P] = np.eye(P)
    mats[:, P:2 * P] = np.triu(np.ones((P, P)), 1)
    mats[:, 2 * P:3 * P] = 1.0
    mats[:, 3 * P:] = np.arange(MAXB)
    inv = np.float32(500000.0) ** (-np.arange(0, ROT, 2, dtype=np.float32) / np.float32(ROT))
    ang = np.arange(SEQ, dtype=np.float32)[:, None] * inv[None, :]
    cos, sin = np.cos(ang), np.sin(ang)
    rope = np.concatenate([cos, cos, -sin, sin], 1).astype(np.float32)
    toks = (np.arange(P)[:, None] + P * np.arange(NT)[None, :]).astype(np.int32)
    rows = np.arange(NE * ROWS_PER_EXPERT)
    pad = np.zeros((NE * ROWS_PER_EXPERT, ENTRY), np.int32)
    pad[:, 0] = rows % P
    pad[:, 1] = SEQ + rows % P
    return {"mats": mats, "rope": rope, "toks": toks, "pad": pad}


_INS = ["x", "g_mix_norm", "w_in", "b_in", "sinks", "gmlp_w_s", "gmlp_b_s", "gmlp_ln_g", "gmlp_ln_b", "g_attn_out",
        "g_gmlp_out", "w_out", "g_ffn_norm", "w_router_group", "b_router_group", "w_router_expert",
        "b_router_expert", "w_gate", "w_up", "w_down", "g_final"]


def kernel(**inputs):
    import concourse.bacc as bacc
    from concourse.bass_utils import run_bass_kernel_spmd

    nc = bacc.Bacc("TRN2", target_bir_lowering=False, num_devices=1)
    arrays, aps = {}, {}
    for name, value in [(n, inputs[n]) for n in _INS] + list(shape_constants().items()):
        value = np.ascontiguousarray(value)
        arrays[f"in_{name}"] = value
        aps[name] = nc.dram_tensor(f"in_{name}", value.shape, mybir.dt.from_np(value.dtype), kind="ExternalInput").ap()
    out = nc.dram_tensor("out", (1, SEQ, D), F32, kind="ExternalOutput").ap()
    build(nc, aps, out)
    result = run_bass_kernel_spmd(nc, [arrays], core_ids=[0])
    return result.results[0]["out"]
```

```python
from contextlib import ExitStack

import numpy as np
import concourse.bass as bass
from concourse import mybir

F32 = mybir.dt.float32
F32R = mybir.dt.float32r
BF16 = mybir.dt.bfloat16
I32 = mybir.dt.int32
U32 = mybir.dt.uint32
ACT = mybir.ActivationFunctionType
ALU = mybir.AluOpType
X = mybir.AxisListType.X

P = 128
SEQ = 4096
D = 1024
NT = SEQ // P
KT = D // P
CHUNK = 64
HD = 64
HEADS = 8
KVH = 2
GRP = HEADS // KVH
ROT = HD // 4
AW = HEADS * HD
KVW = KVH * HD
GG = 8
GC = 64
GW = GG * GC
DIN = AW + 2 * KVW + 2 * GW
V0 = AW + KVW
G0 = AW + 2 * KVW
ZC = [(0, AW), (AW, G0), (G0, G0 + GW), (G0 + GW, DIN)]
NG = 4
EPG = 8
NE = NG * EPG
F = 512
FT = F // P
BLK = 128
EPS = 1e-6
GELU_C = 0.7978845608028654
ROWS_PER_EXPERT = SEQ
MAXB = 2 * NE + 2 * SEQ // BLK + 2
ENTRY = 4
CH, CW = 6, 2048
RAW = 3


def makers(ctx, nc, phase):
    return (lambda n, s, d=F32: ctx.enter_context(nc.sbuf_tensor(f"{phase}_{n}", s, d)),
            lambda n, s: ctx.enter_context(nc.psum_tensor(f"{phase}_{n}", s, F32)),
            lambda n: ctx.enter_context(nc.semaphore(f"{phase}_{n}")))


class Shared:

    def __init__(self, ctx, nc):
        sb, _, sem = makers(ctx, nc, "shared")
        self.ident = sb("ident", [P, P])
        self.raw = [sb(f"raw{s}", [P, CW]) for s in range(RAW)]
        self.ld_ident = sem("ld_ident")
        self.ld_out = [sem(f"ld_out{s}") for s in range(RAW)]
        self.ld_exp = [sem(f"ld_exp{s}") for s in range(RAW)]
        self.st_pad = sem("st_pad")


def w_out_rows(w_out, j):
    return w_out.rearrange("l (k p) n -> (l p) k n", p=P)[:, 2 * j:2 * j + 2, :]


def expert_chunk(w_gate, w_up, w_down, c, e):
    w = (w_gate, w_up, w_down)[c // 2].rearrange("l e (k p) n -> (l e) p k n", p=P)
    half = w.shape[2] // 2
    part = slice((c % 2) * half, (c % 2 + 1) * half)
    return w[bass.ds(e, 1), :, part, :].rearrange("a p k n -> (a p) k n")


def by_rows(slot, width):
    return slot[:].rearrange("p (k n) -> p k n", n=width)


def mixers(nc, shared, x, w_in, b_in, sinks, w_s, b_s, ln_g, ln_b, g_mix, w_out, mats, pad, rope, mix_dram, table):
    with ExitStack() as ctx:
        sb, pb, sem = makers(ctx, nc, "mixers")

        w_hi = sb("w_hi", [P, KT, DIN], F32R)
        w_lo = sb("w_lo", [P, KT, DIN], BF16)
        w_raw = [slot[:, 0:DIN] for slot in shared.raw]
        gmix = sb("gmix", [P, KT])
        bias = sb("bias", [P, DIN])
        ident = shared.ident
        rope_sb = sb("rope_sb", [P, NT, 2, ROT])
        sink = sb("sink", [P, HEADS])
        ws_raw = sb("ws_raw", [P, GG, P])
        wsT = sb("wsT", [P, GG, P])
        bs_sb = sb("bs_sb", [P, GG])
        lng = sb("lng", [P, GW])
        lnb = sb("lnb", [P, GW])
        gate_bias = sb("gate_bias", [P, GW])
        xt = sb("xt", [P, D])
        sq_junk = sb("sq_junk", [P, D])
        ssq = sb("ssq", [P, 1])
        rstd = sb("rstd", [P, 1])
        xT_hi = sb("xT_hi", [P, KT, P], F32R)
        xT_lo = sb("xT_lo", [P, KT, P], F32R)
        xT_b = sb("xT_b", [P, KT, P], BF16)
        z = sb("z", [P, DIN])
        rot1 = sb("rot1", [P, HEADS + KVH, ROT])
        rot2 = sb("rot2", [P, HEADS + KVH, ROT])
        qT = sb("qT", [P, GRP, P])
        kT_cur = sb("kT_cur", [P, P])
        kT_mix = sb("kT_mix", [P, P])
        v_cur = sb("v_cur", [P, KVH, HD + 1])
        v_mix = sb("v_mix", [P, KVH, HD + 1])
        probs = sb("probs", [P, HEADS, P])
        probsT = sb("probsT", [P, HEADS, P])
        mx = sb("mx", [P, HEADS])
        neg_mx = sb("neg_mx", [P, HEADS])
        sink_d = sb("sink_d", [P, HEADS])
        sink_e = sb("sink_e", [P, HEADS])
        den = sb("den", [P, HEADS])
        gel = sb("gel", [P, 2 * GW])
        uv = sb("uv", [P, 2 * GW])
        vsq = sb("vsq", [P, GW])
        st8 = sb("st8", [P, GG])
        mean8 = sb("mean8", [P, GG])
        var8 = sb("var8", [P, GG])
        mix = sb("mix", [P, D])
        nss = sb("nss", [P, 2])
        nrs = sb("nrs", [P, 2])
        minus_half = sb("minus_half", [P, GG])

        ps_z = [pb(f"ps_z{i}", [P, 512]) for i in range(2)]
        ps_t = pb("ps_t", [P, KT, P])
        ps_s = pb("ps_s", [P, HEADS, P])
        ps_o = pb("ps_o", [P, 2, 512])

        ld_w = [sem(f"ld_w{s}") for s in range(RAW)]
        ld_gain = sem("ld_gain")
        ld_gate = sem("ld_gate")
        ld_small = sem("ld_small")
        ld_x = sem("ld_x")
        st_mix = sem("st_mix")
        a_whi = sem("a_whi")
        v_wlo = sem("v_wlo")
        pe_wsT = sem("pe_wsT")
        v_wsT = sem("v_wsT")
        pe_gb = sem("pe_gb")
        v_init = sem("v_init")
        pe_xt = sem("pe_xt")
        pe_z = sem("pe_z")
        pe_qk = sem("pe_qk")
        pe_s = sem("pe_s")
        pe_pt = sem("pe_pt")
        pe_pv = sem("pe_pv")
        pe_sg = sem("pe_sg")
        a_ssq = sem("a_ssq")
        a_xh = sem("a_xh")
        a_gsq = sem("a_gsq")
        a_tanh = sem("a_tanh")
        a_vsq = sem("a_vsq")
        a_exp = sem("a_exp")
        a_pt = sem("a_pt")
        a_qt = sem("a_qt")
        a_nsq = sem("a_nsq")
        a_mix = sem("a_mix")
        v_xb = sem("v_xb")
        v_xl = sem("v_xl")
        v_z = sem("v_z")
        v_rope = sem("v_rope")
        v_kt = sem("v_kt")
        v_vv = sem("v_vv")
        v_gp = sem("v_gp")
        v_cen = sem("v_cen")
        v_max = sem("v_max")
        v_vn = sem("v_vn")
        v_o = sem("v_o")
        v_var = sem("v_var")
        pe_held = sem("pe_held")
        p_held = sem("p_held")
        p_rstd = sem("p_rstd")
        p_var = sem("p_var")
        p_nrs = sem("p_nrs")

        x_t = x.rearrange("b (t p) d -> (b t) p d", p=P)
        mix_t = mix_dram.rearrange("(t p) d -> t p d", p=P)
        w_in_t = w_in.rearrange("l (k p) n -> (l k) p n", p=P)
        N_GATE, N_SMALL = 3, 4

        block = ctx.enter_context(nc.Block())

        @block.sync
        def _(sp):
            sp.dma_start(xt[:], x_t[0]).then_inc(ld_x, 16)
            sp.dma_start(ident[:], mats[:, 0:P]).then_inc(shared.ld_ident, 16)
            sp.dma_start(gmix[:], g_mix.rearrange("l (k p) -> p (l k)", p=P),
                         allow_slow_non_contiguous=True).then_inc(ld_gain, 16)
            for k in range(KT):
                if k >= RAW:
                    sp.wait_ge(v_wlo, k - RAW + 1)
                sp.dma_start(w_raw[k % RAW], w_in_t[k]).then_inc(ld_w[k % RAW], 16)
                if k == RAW - 1:
                    sp.dma_start(ws_raw[:], w_s.rearrange("l g i j -> i (l g) j")).then_inc(ld_gate, 16)
                    sp.dma_start(bs_sb[:], b_s.rearrange("l g i -> i (l g)"), allow_slow_non_contiguous=True).then_inc(ld_gate, 16)
                    sp.dma_start(lnb[:], ln_b.rearrange("l g c -> l (g c)").to_broadcast((P, GW))).then_inc(ld_gate, 16)
            sp.dma_start(bias[:], b_in.to_broadcast((P, DIN))).then_inc(ld_small, 16)
            sp.dma_start(rope_sb[:].rearrange("p t a c -> p t (a c)"),
                         rope.rearrange("(t p) c -> p t c", p=P)).then_inc(ld_small, 16)
            sp.dma_start(sink[:], sinks.to_broadcast((P, HEADS))).then_inc(ld_small, 16)
            sp.dma_start(lng[:], ln_g.rearrange("l g c -> l (g c)").to_broadcast((P, GW))).then_inc(ld_small, 16)

            def load_x(n):
                sp.wait_ge(pe_xt, n)
                sp.wait_ge(a_ssq, n)
                sp.dma_start(xt[:], x_t[bass.ds(n, 1)].rearrange("a p d -> (a p) d")).then_inc(ld_x, 16)

            def store_mix(m):
                sp.wait_ge(a_mix, m + 1)
                sp.dma_start(mix_t[bass.ds(m, 1)].rearrange("a p d -> (a p) d"), mix[:]).then_inc(st_mix, 16)

            load_x(1)
            load_x(2)
            sp.wait_ge(v_wlo, KT)
            for j in range(RAW):
                sp.dma_start(by_rows(shared.raw[j], D), w_out_rows(w_out, j)).then_inc(shared.ld_out[j], 16)
            sp.dma_start(table.rearrange("(p j) c -> p (j c)", p=P),
                         pad.rearrange("(p j) c -> p (j c)", p=P)).then_inc(shared.st_pad, 16)
            load_x(3)
            store_mix(0)
            with sp.Fori(2, NT - 2) as i:
                load_x(i + 2)
                store_mix(i - 1)
            store_mix(NT - 3)
            store_mix(NT - 2)
            store_mix(NT - 1)
            sp.wait_ge(st_mix, 16 * NT)

        @block.tensor
        def _(pe):
            def x_transposes(n, prior_qk):
                pe.wait_ge(ld_x, 16 * (n + 1))
                if prior_qk:
                    pe.wait_ge(a_qt, n - 1)
                    pe.wait_ge(v_kt, n - 1)
                for k in range(KT):
                    last = nc.tensor.transpose(ps_t[:, k, :], xt[:, k * P:(k + 1) * P], ident[:])
                last.then_inc(pe_xt, 1)

            def z_chunk(i, c, reused, first=False):
                if c == 0:
                    pe.wait_ge(v_xb, i + 1)
                if reused:
                    pe.wait_ge(v_z, 4 * i + c - 1)
                a, b = ZC[c]
                out = ps_z[c % 2][:, 0:b - a]
                for k in range(KT):
                    if first:
                        pe.wait_ge(v_wlo, k + 1)
                    nc.tensor.matmul(out, xT_hi[:, k, :], w_hi[:, k, a:b], start=(k == 0), stop=False)
                    nc.tensor.matmul(out, xT_lo[:, k, :], w_hi[:, k, a:b], start=False, stop=False)
                    last = nc.tensor.matmul(out, xT_b[:, k, :], w_lo[:, k, a:b], start=False, stop=(k == KT - 1))
                last.then_inc(pe_z, 1)

            def scores(m, first):
                pe.wait_ge(a_qt, m + 1)
                pe.wait_ge(v_kt, m + 1)
                if not first:
                    pe.wait_ge(v_o, m)
                pe.sem_inc(pe_held, 1)
                for h in range(HEADS):
                    rows = slice(HD * (h // GRP), HD * (h // GRP) + HD)
                    for c, keys in ((0, kT_mix), (1, kT_cur)):
                        last = nc.tensor.matmul(ps_s[c * CHUNK:(c + 1) * CHUNK, h, :],
                                                qT[rows, h % GRP, c * CHUNK:(c + 1) * CHUNK], keys[rows, :],
                                                start=True, stop=True)
                last.then_inc(pe_s, 1)

            def prob_transposes(m):
                pe.wait_ge(a_exp, m + 1)
                for h in range(HEADS):
                    last = nc.tensor.transpose(ps_s[:, h, :], probs[:, h, :], ident[:])
                last.then_inc(pe_pt, 1)

            def attend(m):
                pe.wait_ge(a_pt, m + 1)
                pe.wait_ge(v_vv, m + 1)
                for h in range(HEADS):
                    o = (h % GRP) * (HD + 1)
                    for c, vals in ((0, v_mix), (1, v_cur)):
                        last = nc.tensor.matmul(ps_o[c * CHUNK:(c + 1) * CHUNK, h // GRP, o:o + HD + 1],
                                                probsT[:, h, c * CHUNK:(c + 1) * CHUNK], vals[:, h // GRP, :],
                                                start=True, stop=True)
                last.then_inc(pe_pv, 1)

            def gating(m):
                pe.wait_ge(v_vn, m + 1)
                for g in range(GG):
                    last = nc.tensor.matmul(ps_s[:, g // 2, (g % 2) * GC:(g % 2 + 1) * GC], wsT[:, g, :],
                                            uv[:, GW + g * GC:GW + (g + 1) * GC], start=True, stop=True)
                last.then_inc(pe_sg, 1)

            def qk_transposes(i, prior_x):
                pe.wait_ge(v_rope, i + 1)
                if prior_x:
                    pe.wait_ge(v_xl, i + 2)
                for b in range(GRP):
                    nc.tensor.transpose(ps_t[:, b, :], z[:, b * P:(b + 1) * P], ident[:])
                nc.tensor.transpose(ps_t[:, GRP, :], z[:, AW:AW + KVW], ident[:]).then_inc(pe_qk, 1)

            def step(i, a, b, nx, first, second):
                if a:
                    z_chunk(i, 0, not first, first)
                if b:
                    if second:
                        pe.wait_ge(v_init, 1)
                    scores(i - 1, second)
                if a:
                    z_chunk(i, 1, not first)
                    z_chunk(i, 2, True)
                if b:
                    prob_transposes(i - 1)
                if nx:
                    x_transposes(i + 1, not first)
                if a:
                    z_chunk(i, 3, True)
                if b:
                    attend(i - 1)
                    gating(i - 1)
                if a:
                    qk_transposes(i, nx)

            pe.wait_ge(shared.ld_ident, 16)
            x_transposes(0, False)
            pe.wait_ge(ld_gate, 16 * N_GATE)
            for g in range(GG):
                last = nc.tensor.transpose(ps_s[:, g, :], ws_raw[:, g, :], ident[:])
            last.then_inc(pe_wsT, 1)
            pe.wait_ge(v_wsT, 1)
            for g in range(GG):
                last = nc.tensor.matmul(ps_s[:, g // 2, (g % 2) * GC:(g % 2 + 1) * GC], wsT[:, g, :],
                                        lnb[:, g * GC:(g + 1) * GC], start=True, stop=True)
            last.then_inc(pe_gb, 1)
            step(0, True, False, True, True, False)
            step(1, True, True, True, False, True)
            with pe.Fori(2, NT - 1) as i:
                step(i, True, True, True, False, False)
            step(NT - 1, True, True, False, False, False)
            step(NT, False, True, False, False, False)

        @block.scalar
        def _(act):
            def square_x(n, first):
                act.wait_ge(ld_x, 16 * (n + 1))
                if not first:
                    act.wait_ge(p_rstd, n)
                nc.scalar.activation(sq_junk[:], xt[:], ACT.Square, accum_out=ssq[:]).then_inc(a_ssq, 1)

            def split_x(n, first):
                if not first:
                    act.wait_ge(pe_z, 4 * n)
                act.wait_ge(pe_xt, n + 1)
                nc.scalar.copy(xT_hi[:], ps_t[:]).then_inc(a_xh, 1)

            def step(i, a, b, nx, first):
                m = i - 1
                if b:
                    act.wait_ge(v_gp, m + 1)
                    nc.scalar.activation(gel[:], gel[:], ACT.Tanh, scale=GELU_C).then_inc(a_tanh, 1)
                    act.wait_ge(v_cen, m + 1)
                    nc.scalar.activation(vsq[:], uv[:, GW:2 * GW], ACT.Square).then_inc(a_vsq, 1)
                    act.wait_ge(v_max, m + 1)
                    for h in range(HEADS):
                        nc.scalar.activation(probs[:, h, :], ps_s[:, h, :], ACT.Exp, bias=neg_mx[:, h:h + 1])
                    nc.scalar.activation(sink_e[:], sink_d[:], ACT.Exp).then_inc(a_exp, 1)
                    act.wait_ge(pe_pt, m + 1)
                    nc.scalar.copy(probsT[:], ps_s[:]).then_inc(a_pt, 1)
                if nx:
                    square_x(i + 1, False)
                    split_x(i + 1, False)
                if a:
                    act.wait_ge(pe_qk, i + 1)
                    nc.scalar.mul(qT[:], ps_t[:, 0:GRP, :], HD ** -0.5).then_inc(a_qt, 1)
                    act.wait_ge(v_z, 4 * i + 4)
                    if not first:
                        act.wait_ge(v_cen, i)
                    nc.scalar.activation(gel[:], z[:, G0:DIN], ACT.Square).then_inc(a_gsq, 1)
                if b:
                    act.wait_ge(v_o, m + 1)
                    nc.scalar.activation(sq_junk[:, 0:AW], mix[:, 0:AW], ACT.Square, accum_out=nss[:, 0:1])
                    nc.scalar.activation(sq_junk[:, AW:D], mix[:, AW:D], ACT.Square, accum_out=nss[:, 1:2]).then_inc(a_nsq, 1)
                    act.wait_ge(p_nrs, m + 1)
                    nc.scalar.mul(mix[:, 0:AW], mix[:, 0:AW], nrs[:, 0:1])
                    nc.scalar.mul(mix[:, AW:D], mix[:, AW:D], nrs[:, 1:2]).then_inc(a_mix, 1)

            square_x(0, True)
            split_x(0, True)
            act.wait_ge(ld_gain, 16)
            for k in range(KT):
                act.wait_ge(ld_w[k % RAW], 16 * (k // RAW + 1))
                nc.scalar.mul(w_hi[:, k, :], w_raw[k % RAW], gmix[:, k:k + 1]).then_inc(a_whi, 1)
            step(0, True, False, True, True)
            step(1, True, True, True, False)
            with act.Fori(2, NT - 1) as i:
                step(i, True, True, True, False)
            step(NT - 1, True, True, False, False)
            step(NT, False, True, False, False)

        @block.vector
        def _(dve):
            V = nc.vector

            def split_x(n, first):
                dve.wait_ge(a_xh, n + 1)
                if not first:
                    dve.wait_ge(pe_z, 4 * n)
                V.tensor_tensor(xT_lo[:], ps_t[:], xT_hi[:].bitcast(F32), ALU.subtract).then_inc(v_xl, 1)
                V.tensor_copy(xT_b[:], xT_hi[:].bitcast(F32)).then_inc(v_xb, 1)

            def z_chunk(i, c):
                dve.wait_ge(pe_z, 4 * i + c + 1)
                a, b = ZC[c]
                if c == 0:
                    placed = z[:, 0:AW].rearrange("p (h k d) -> p k h d", k=KVH, d=HD)
                    for kv in range(KVH):
                        cols = slice(kv * AW // KVH, (kv + 1) * AW // KVH)
                        last = V.scalar_tensor_tensor(placed[:, kv], ps_z[0][:, cols].rearrange("p (h d) -> p h d", d=HD),
                                                      rstd[:], bias[:, cols].rearrange("p (h d) -> p h d", d=HD),
                                                      ALU.mult, ALU.add)
                    last.then_inc(v_z, 1)
                    return
                V.scalar_tensor_tensor(z[:, a:b], ps_z[c % 2][:, 0:b - a], rstd[:], bias[:, a:b],
                                       ALU.mult, ALU.add).then_inc(v_z, 1)

            def rope_qk(i):
                heads = z[:, 0:AW + KVW].rearrange("p (h d) -> p h d", d=HD)
                both = (P, HEADS + KVH, ROT)
                half = (P, HEADS + KVH, ROT // 2)
                table = rope_sb[:, bass.ds(i, 1), :, :].rearrange("p t a c -> p (t a) c")
                V.drain()
                V.tensor_tensor(rot1[:], heads[:, :, 0:ROT], table[:, 0:1, :].to_broadcast(both), ALU.mult)
                V.tensor_tensor(rot2[:, :, 0:ROT // 2], heads[:, :, ROT // 2:ROT],
                                table[:, 1:2, 0:ROT // 2].to_broadcast(half), ALU.mult)
                V.tensor_tensor(rot2[:, :, ROT // 2:ROT], heads[:, :, 0:ROT // 2],
                                table[:, 1:2, ROT // 2:ROT].to_broadcast(half), ALU.mult)
                V.drain()
                V.tensor_tensor(heads[:, :, 0:ROT], rot1[:], rot2[:], ALU.add).then_inc(v_rope, 1)

            def step(i, a, b, nx, first, second):
                m = i - 1
                vv = uv[:, GW:2 * GW].rearrange("p (g c) -> p g c", c=GC)
                per_group = (P, GG, GC)
                if b:
                    dve.wait_ge(a_gsq, m + 1)
                    V.tensor_scalar(gel[:], gel[:], 0.044715, 1.0, ALU.mult, ALU.add)
                    V.drain()
                    V.tensor_tensor(gel[:], gel[:], z[:, G0:DIN], ALU.mult).then_inc(v_gp, 1)
                if a:
                    dve.wait_ge(p_rstd, i + 1)
                    z_chunk(i, 0)
                if b:
                    dve.wait_ge(a_tanh, m + 1)
                    V.scalar_tensor_tensor(uv[:], gel[:], 1.0, z[:, G0:DIN], ALU.add, ALU.mult)
                    V.drain()
                    V.reduce_sum(st8[:], vv, axis=X)
                    V.drain()
                    V.tensor_scalar(mean8[:], st8[:], 1.0 / GC, None, ALU.mult)
                    V.drain()
                    V.tensor_tensor(vv, vv, mean8[:].unsqueeze(2).to_broadcast(per_group), ALU.subtract).then_inc(v_cen, 1)
                    dve.wait_ge(pe_s, m + 1)
                    V.reduce_max(mx[:], ps_s[:], axis=X)
                    V.drain()
                    V.tensor_tensor(mx[:], mx[:], sink[:], ALU.max)
                    V.drain()
                    V.tensor_scalar(neg_mx[:], mx[:], -1.0, None, ALU.mult)
                    V.tensor_tensor(sink_d[:], sink[:], mx[:], ALU.subtract).then_inc(v_max, 1)
                    dve.wait_ge(a_vsq, m + 1)
                    V.reduce_sum(var8[:], vsq[:].rearrange("p (g c) -> p g c", c=GC), axis=X).then_inc(v_var, 1)
                if a:
                    z_chunk(i, 1)
                    rope_qk(i)
                if b:
                    dve.wait_ge(p_var, m + 1)
                    V.tensor_tensor(vv, vv, var8[:].unsqueeze(2).to_broadcast(per_group), ALU.mult).then_inc(v_vn, 1)
                if a:
                    z_chunk(i, 2)
                if nx:
                    split_x(i + 1, False)
                if a:
                    z_chunk(i, 3)
                if b:
                    dve.wait_ge(pe_pv, m + 1)
                    dve.wait_ge(a_exp, m + 1)
                    if not second:
                        dve.wait_ge(st_mix, 16 * m)
                    o = ps_o[:, :, 0:GRP * (HD + 1)].rearrange("p k (h d) -> p k h d", d=HD + 1)
                    den3 = den[:].rearrange("p (k h) -> p k h", k=KVH)
                    V.tensor_tensor(den3, o[:, :, :, HD], sink_e[:].rearrange("p (k h) -> p k h", k=KVH), ALU.add)
                    V.drain()
                    V.reciprocal(den[:], den[:])
                    V.drain()
                    for kv in range(KVH):
                        V.tensor_tensor(mix[:, kv * 256:(kv + 1) * 256].rearrange("p (h d) -> p h d", d=HD),
                                        o[:, kv, :, 0:HD],
                                        den3[:, kv, :].unsqueeze(2).to_broadcast((P, GRP, HD)), ALU.mult)
                    dve.wait_ge(pe_sg, m + 1)
                    mo = mix[:, AW:D]
                    V.tensor_tensor(mo, ps_s[:, 0:GRP, :].rearrange("p a b -> p (a b)"), lng[:], ALU.mult)
                    V.drain()
                    V.tensor_tensor(mo, mo, gate_bias[:], ALU.add)
                    V.drain()
                    V.scalar_tensor_tensor(mo, uv[:, 0:GW], 0.5, mo, ALU.mult, ALU.mult).then_inc(v_o, 1)
                if a:
                    dve.wait_ge(pe_qk, i + 1)
                    if first:
                        V.tensor_copy(kT_mix[:, CHUNK:P], ps_t[:, GRP, 0:CHUNK])
                    else:
                        V.tensor_copy(kT_mix[:, CHUNK:P], kT_cur[:, CHUNK:P])
                    V.tensor_copy(kT_mix[:, 0:CHUNK], ps_t[:, GRP, 0:CHUNK])
                    V.drain()
                    V.tensor_copy(kT_cur[:], ps_t[:, GRP, :]).then_inc(v_kt, 1)
                    zv = z[:, V0:G0].rearrange("p (k d) -> p k d", d=HD)
                    if not first:
                        V.tensor_copy(v_mix[CHUNK:P], v_cur[CHUNK:P])
                    V.tensor_copy(v_mix[0:CHUNK, :, 0:HD], zv[0:CHUNK])
                    V.drain()
                    V.tensor_copy(v_cur[:, :, 0:HD], zv).then_inc(v_vv, 1)

            V.memset(v_cur[:], 1.0)
            V.memset(v_mix[0:CHUNK], 1.0)
            V.memset(v_mix[CHUNK:P], 0.0)
            split_x(0, True)
            for k in range(KT):
                dve.wait_ge(a_whi, k + 1)
                V.scalar_tensor_tensor(w_lo[:, k, :], w_raw[k % RAW], gmix[:, k:k + 1], w_hi[:, k, :].bitcast(F32),
                                       ALU.mult, ALU.subtract).then_inc(v_wlo, 1)
                if k == RAW:
                    dve.wait_ge(pe_wsT, 1)
                    V.tensor_copy(wsT[:], ps_s[:])
                    V.drain()
                    V.memset(wsT[CHUNK:P, :, 0:CHUNK], 0.0)
                    V.drain().then_inc(v_wsT, 1)
                if k == RAW + 2:
                    dve.wait_ge(pe_gb, 1)
                    V.tensor_tensor(gate_bias[:].rearrange("p (g c) -> p g c", c=GC),
                                    ps_s[:, 0:GRP, :].rearrange("p a (b c) -> p (a b) c", c=GC),
                                    bs_sb[:].unsqueeze(2).to_broadcast((P, GG, GC)), ALU.add).then_inc(v_init, 1)
            dve.wait_ge(ld_small, 16 * N_SMALL)
            step(0, True, False, True, True, False)
            step(1, True, True, True, False, True)
            with dve.Fori(2, NT - 1) as i:
                step(i, True, True, True, False, False)
            step(NT - 1, True, True, False, False, False)
            step(NT, False, True, False, False, False)

        @block.gpsimd
        def _(pool):
            def inverse_root(out, sums, n, eps=EPS):
                nc.gpsimd.tensor_scalar(out, sums, 1.0 / n, eps, ALU.mult, ALU.add)
                nc.gpsimd.drain()
                return nc.gpsimd.tensor_tensor(out, out, minus_half[:, 0:out.shape[1]], ALU.pow)

            def norm_x(n, first):
                if not first:
                    pool.wait_ge(v_z, 4 * n)
                pool.wait_ge(a_ssq, n + 1)
                pool.sem_inc(p_held, 1)
                inverse_root(rstd[:], ssq[:], D).then_inc(p_rstd, 1)

            def step(m, nx):
                pool.wait_ge(v_var, m + 1)
                pool.sem_inc(p_held, 1)
                inverse_root(var8[:], var8[:], GC, 4 * EPS).then_inc(p_var, 1)
                if nx:
                    norm_x(m + 2, False)
                pool.wait_ge(a_nsq, m + 1)
                pool.sem_inc(p_held, 1)
                inverse_root(nrs[:], nss[:], AW).then_inc(p_nrs, 1)

            nc.gpsimd.memset(minus_half[:], -0.5)
            nc.gpsimd.drain()
            norm_x(0, True)
            norm_x(1, False)
            with pool.Fori(0, NT - 2) as m:
                step(m, True)
            step(NT - 2, False)
            step(NT - 1, False)


def after(engine, semaphore, count):
    if not isinstance(count, int) or count > 0:
        engine.wait_ge(semaphore, count)


def within(i, low, high):
    return not isinstance(i, int) or low <= i <= high


def project(nc, shared, x, mix_dram, w_out, g_attn, g_gmlp, g_ffn, w_rg, b_rg, w_re, b_re, mats, toks,
            w_gate, w_up, w_down, h_dram, hn_dram, table, bstart, brow):
    NR = NG + NE
    NEG = -3.0e38
    with ExitStack() as ctx:
        sb, pb, sem = makers(ctx, nc, "project")

        wo_hi = sb("wo_hi", [P, KT, D], F32R)
        wo_lo = sb("wo_lo", [P, KT, D], BF16)
        gains = sb("gains", [P, KT])
        gffn = sb("gffn", [P, D])
        mats_sb = sb("mats_sb", [P, 3 * P + MAXB])
        ident = shared.ident[:]
        iota = mats_sb[:, 3 * P:3 * P + NE]
        iota_b = mats_sb[:, 3 * P:3 * P + MAXB]
        before = sb("before", [P, P], BF16)
        ones = sb("ones", [P, P], BF16)
        toks_sb = sb("toks_sb", [P, NT], I32)
        w_r = sb("w_r", [P, KT, NR])
        b_r = sb("b_r", [P, NR])
        zero = sb("zero", [P, D])
        mixt = sb("mixt", [P, D])
        mT_hi = sb("mT_hi", [P, KT, P], F32R)
        mT_lo = sb("mT_lo", [P, KT, P], F32R)
        mT_b = sb("mT_b", [P, KT, P], BF16)
        xt = sb("xt", [P, D])
        h = sb("h", [P, D])
        hn = sb("hn", [P, D])
        hnT = sb("hnT", [P, KT, P])
        junk = sb("junk", [P, D])
        ssq = sb("ssq", [P, 1])
        rstd = sb("rstd", [P, 1])
        minus_half = sb("minus_half", [P, 1])
        lg = sb("lg", [P, 8])
        le = sb("le", [P, NE])
        gtop = sb("gtop", [P, 8])
        gidx = sb("gidx", [P, 8], U32)
        gidx_f = sb("gidx_f", [P, 1])
        gbase = sb("gbase", [P, 1])
        neg_g = sb("neg_g", [P, 1])
        goh = sb("goh", [P, NG])
        lsel = sb("lsel", [P, NG, EPG])
        esel = sb("esel", [P, EPG])
        etop = sb("etop", [P, 8])
        eidx = sb("eidx", [P, 8], U32)
        neg_e = sb("neg_e", [P, 1])
        eid = sb("eid", [P, 2])
        oh = sb("oh", [P, 2, NE])
        oh_sum = sb("oh_sum", [P, NE], BF16)
        oh_acc = sb("oh_acc", [P, NE], BF16)
        gjunk = sb("gjunk", [P, NG])
        gsum = sb("gsum", [P, 1])
        ed = sb("ed", [P, 1])
        wden = sb("wden", [P, 1])
        wts = sb("wts", [P, 2])
        rk = sb("rk", [P, 2, NE])
        rank = sb("rank", [P, 2])
        dest_f = sb("dest_f", [P, 2])
        dest = sb("dest", [P, 2], I32)
        entry = sb("entry", [P, 2, ENTRY], I32)
        cnt_i = sb("cnt_i", [NE, 1], I32)
        upto = sb("upto", [P, NE])
        blocks = sb("blocks", [NE, 1])
        end = sb("end", [NE, 1])
        skip = sb("skip", [NE, 1])
        ended = sb("ended", [NE, MAXB])
        first_row = sb("first_row", [1, MAXB])

        ps_t = pb("ps_t", [P, KT, P])
        ps_y = pb("ps_y", [P, D])
        ps_h = pb("ps_h", [P, KT, P])
        ps_r = pb("ps_r", [P, 512])
        ps_k = pb("ps_k", [P, 512])

        ld_gain = sem("ld_gain")
        ld_small = sem("ld_small")
        ld_mix = sem("ld_mix")
        ld_x = sem("ld_x")
        st_h = sem("st_h")
        st_hn = sem("st_hn")
        st_past = sem("st_past")
        st_ent = sem("st_ent")
        a_whi = sem("a_whi")
        v_wlo = sem("v_wlo")
        v_init = sem("v_init")
        pe_mt = sem("pe_mt")
        pe_y = sem("pe_y")
        pe_ht = sem("pe_ht")
        pe_r = sem("pe_r")
        pe_rk = sem("pe_rk")
        a_mh = sem("a_mh")
        a_hsq = sem("a_hsq")
        a_ht = sem("a_ht")
        a_ex = sem("a_ex")
        p_rstd = sem("p_rstd")
        p_held = sem("p_held")
        v_ml = sem("v_ml")
        v_h = sem("v_h")
        v_hn = sem("v_hn")
        v_g = sem("v_g")
        v_oh = sem("v_oh")
        v_ent = sem("v_ent")
        v_acc = sem("v_acc")
        v_blocks = sem("v_blocks")
        v_ended = sem("v_ended")
        pe_cnt = sem("pe_cnt")
        pe_end = sem("pe_end")
        pe_row = sem("pe_row")

        x_t = x.rearrange("b (t p) d -> (b t) p d", p=P)
        mix_t = mix_dram.rearrange("(t p) d -> t p d", p=P)
        h_t = h_dram.rearrange("(t p) d -> t p d", p=P)
        hn_t = hn_dram.rearrange("(t p) d -> t p d", p=P)
        N_SMALL = 7
        HALF = KT // 2

        block = ctx.enter_context(nc.Block())
        STEADY = (4, NT - 2)
        STEPS = NT + 3

        def all_steps(engine, step):
            for i in range(STEADY[0]):
                step(i)
            with engine.Fori(*STEADY) as i:
                step(i)
            for i in range(STEADY[1], STEPS):
                step(i)

        @block.sync
        def _(sp):
            def load_mix(n):
                after(sp, pe_mt, n)
                sp.dma_start(mixt[:], mix_t[bass.ds(n, 1)].rearrange("a p d -> (a p) d")).then_inc(ld_mix, 16)

            def load_x(n):
                after(sp, v_h, n)
                sp.dma_start(xt[:], x_t[bass.ds(n, 1)].rearrange("a p d -> (a p) d")).then_inc(ld_x, 16)

            def step(i):
                if within(i, 1, NT):
                    m = i - 1
                    sp.wait_ge(v_h, m + 1)
                    sp.dma_start(h_t[bass.ds(m, 1)].rearrange("a p d -> (a p) d"), h[:]).then_inc(st_h, 16)
                    if within(i, 1, NT - 1):
                        load_x(i)
                    sp.wait_ge(v_hn, m + 1)
                    sp.dma_start(hn_t[bass.ds(m, 1)].rearrange("a p d -> (a p) d"), hn[:]).then_inc(st_hn, 16)
                if within(i, 0, NT - 3):
                    load_mix(i + 2)

            for n, g in enumerate((g_attn, g_gmlp)):
                sp.dma_start(gains[:, n * HALF:(n + 1) * HALF], g.rearrange("l (k p) -> p (l k)", p=P),
                             allow_slow_non_contiguous=True).then_inc(ld_gain, 16)
            load_mix(0)
            load_x(0)
            load_mix(1)
            sp.dma_start(gffn[:], g_ffn.to_broadcast((P, D))).then_inc(ld_small, 16)
            sp.dma_start(mats_sb[:], mats).then_inc(ld_small, 16)
            for j in range(RAW, KT // 2):
                sp.wait_ge(v_wlo, 2 * (j - RAW) + 2)
                sp.dma_start(by_rows(shared.raw[j % RAW], D), w_out_rows(w_out, j)).then_inc(shared.ld_out[j % RAW], 16)
            sp.dma_start(toks_sb[:], toks).then_inc(ld_small, 16)
            sp.dma_start(w_r[:, :, 0:NG], w_rg.rearrange("l (k p) n -> p (l k) n", p=P)).then_inc(ld_small, 16)
            sp.dma_start(w_r[:, :, NG:NR], w_re.rearrange("l (k p) n -> p (l k) n", p=P)).then_inc(ld_small, 16)
            sp.dma_start(b_r[:, 0:NG], b_rg.to_broadcast((P, NG))).then_inc(ld_small, 16)
            sp.dma_start(b_r[:, NG:NR], b_re.to_broadcast((P, NE))).then_inc(ld_small, 16)
            sp.wait_ge(v_wlo, KT)
            for c in range(RAW):
                sp.dma_start(by_rows(shared.raw[c], F if c < 4 else D),
                             expert_chunk(w_gate, w_up, w_down, c, 0)).then_inc(shared.ld_exp[c], 16)
            sp.wait_ge(v_init, 1)
            sp.dma_start(h_t[NT], zero[:]).then_inc(st_past, 16)
            all_steps(sp, step)
            sp.wait_ge(st_h, 16 * NT)
            sp.wait_ge(st_hn, 16 * NT)
            sp.wait_ge(st_past, 16)

        @block.tensor
        def _(pe):
            def mix_transposes(n):
                pe.wait_ge(ld_mix, 16 * (n + 1))
                after(pe, v_ml, 2 * n)
                for k in range(KT):
                    last = nc.tensor.transpose(ps_t[:, k, :], mixt[:, k * P:(k + 1) * P], ident)
                last.then_inc(pe_mt, 1)

            def half_product(i, half):
                pe.wait_ge(v_ml, 2 * i + half + 1)
                for k in range(half * HALF, (half + 1) * HALF):
                    if isinstance(i, int) and i == 0:
                        pe.wait_ge(v_wlo, k + 1)
                    for c in range(2):
                        out, cols = ps_y[:, c * 512:(c + 1) * 512], slice(c * 512, (c + 1) * 512)
                        nc.tensor.matmul(out, mT_hi[:, k, :], wo_hi[:, k, cols], start=(k == 0), stop=False)
                        nc.tensor.matmul(out, mT_lo[:, k, :], wo_hi[:, k, cols], start=False, stop=False)
                        last = nc.tensor.matmul(out, mT_b[:, k, :], wo_lo[:, k, cols], start=False, stop=(k == KT - 1))
                last.then_inc(pe_y, 1)

            def step(i):
                m, r = i - 1, i - 2
                if within(i, 0, NT - 1):
                    after(pe, v_h, i)
                    half_product(i, 0)
                if within(i, 0, NT - 2):
                    mix_transposes(i + 1)
                if within(i, 1, NT):
                    pe.wait_ge(v_hn, m + 1)
                    after(pe, a_ht, m)
                    for k in range(KT):
                        last = nc.tensor.transpose(ps_h[:, k, :], hn[:, k * P:(k + 1) * P], ident)
                    last.then_inc(pe_ht, 1)
                if within(i, 0, NT - 1):
                    half_product(i, 1)
                if within(i, 1, NT):
                    if isinstance(i, int) and i == 1:
                        pe.wait_ge(v_init, 1)
                    pe.wait_ge(a_ht, m + 1)
                    after(pe, v_oh, m)
                    for k in range(KT):
                        last = nc.tensor.matmul(ps_r[:, 0:NR], hnT[:, k, :], w_r[:, k, :], start=(k == 0), stop=(k == KT - 1))
                    last.then_inc(pe_r, 1)
                if within(i, 2, NT + 1):
                    pe.wait_ge(v_oh, r + 1)
                    after(pe, v_ent, r)
                    nc.tensor.matmul(ps_k[:, 0:NE], before[:], oh_sum[:], start=True, stop=False)
                    nc.tensor.matmul(ps_k[:, 0:NE], ones[:], oh_acc[:], start=False, stop=True).then_inc(pe_rk, 1)

            mix_transposes(0)
            all_steps(pe, step)
            pe.wait_ge(v_acc, 1)
            nc.tensor.matmul(ps_k[0:NE, 0:1], oh_acc[:], ones[:, 0:1], start=True, stop=True).then_inc(pe_cnt, 1)
            pe.wait_ge(v_blocks, 1)
            nc.tensor.matmul(ps_k[0:NE, 1:2], upto[0:NE, :], blocks[:], start=True, stop=True)
            nc.tensor.matmul(ps_r[0:1, 0:NE], blocks[:], upto[0:NE, :], start=True, stop=True).then_inc(pe_end, 1)
            pe.wait_ge(v_ended, 1)
            nc.tensor.matmul(ps_y[0:1, 0:MAXB], skip[:], ended[:], start=True, stop=True).then_inc(pe_row, 1)

        @block.scalar
        def _(act):
            def split_half(n, half):
                act.wait_ge(pe_mt, n + 1)
                after(act, pe_y, 2 * n - 1 + half)
                ks = slice(half * HALF, (half + 1) * HALF)
                nc.scalar.copy(mT_hi[:, ks, :], ps_t[:, ks, :]).then_inc(a_mh, 1)

            def step(i):
                m, r = i - 1, i - 2
                if within(i, 1, NT - 1):
                    split_half(i, 1)
                if within(i, 1, NT):
                    act.wait_ge(v_h, m + 1)
                    after(act, p_rstd, m)
                    nc.scalar.activation(junk[:], h[:], ACT.Square, accum_out=ssq[:]).then_inc(a_hsq, 1)
                if within(i, 0, NT - 2):
                    split_half(i + 1, 0)
                if within(i, 1, NT):
                    act.wait_ge(pe_ht, m + 1)
                    after(act, pe_r, m)
                    nc.scalar.copy(hnT[:], ps_h[:]).then_inc(a_ht, 1)
                if within(i, 2, NT + 1):
                    act.wait_ge(v_g, r + 1)
                    nc.scalar.activation(gjunk[:], lg[:, 0:NG], ACT.Exp, bias=neg_g[:], accum_out=gsum[:])
                    nc.scalar.activation(ed[:], etop[:, 1:2], ACT.Exp, bias=neg_e[:]).then_inc(a_ex, 1)

            act.wait_ge(ld_gain, 32)
            for k in range(KT):
                j = k // 2
                act.wait_ge(shared.ld_out[j % RAW], 16 * (j // RAW + 1))
                nc.scalar.mul(wo_hi[:, k, :], by_rows(shared.raw[j % RAW], D)[:, k % 2], gains[:, k:k + 1]).then_inc(a_whi, 1)
                if k in (2, 4):
                    split_half(0, (k - 2) // 2)
            all_steps(act, step)

        @block.vector
        def _(dve):
            V = nc.vector

            def split_half(n, half):
                dve.wait_ge(a_mh, 2 * n + half + 1)
                after(dve, pe_y, 2 * n - 1 + half)
                ks = slice(half * HALF, (half + 1) * HALF)
                V.tensor_copy(mT_b[:, ks, :], mT_hi[:, ks, :].bitcast(F32))
                V.tensor_tensor(mT_lo[:, ks, :], ps_t[:, ks, :], mT_hi[:, ks, :].bitcast(F32), ALU.subtract).then_inc(v_ml, 1)

            def entries(s):
                dve.wait_ge(pe_rk, s + 1)
                V.tensor_tensor(rk[:], oh[:], ps_k[:, 0:NE].unsqueeze(1).to_broadcast((P, 2, NE)), ALU.mult)
                V.tensor_tensor(oh_acc[:], oh_acc[:], oh_sum[:], ALU.add)
                V.drain()
                V.reduce_sum(rank[:], rk[:], axis=X)
                V.drain()
                V.scalar_tensor_tensor(dest_f[:], eid[:], float(ROWS_PER_EXPERT), rank[:], ALU.mult, ALU.add)
                after(dve, st_ent, 32 * s)
                for k in range(2):
                    for c in range(2):
                        V.tensor_copy(entry[:, k, c:c + 1], toks_sb[:, bass.ds(s, 1)])
                V.tensor_copy(entry[:, :, 2].bitcast(F32), wts[:])
                V.drain()
                V.tensor_copy(dest[:], dest_f[:]).then_inc(v_ent, 1)

            def route(r):
                dve.wait_ge(pe_r, r + 1)
                V.tensor_tensor(lg[:, 0:NG], ps_r[:, 0:NG], b_r[:, 0:NG], ALU.add)
                V.tensor_tensor(le[:], ps_r[:, NG:NR], b_r[:, NG:NR], ALU.add)
                V.drain()
                V.max(gtop[:], lg[:])
                V.drain()
                V.max_index(gidx[:], gtop[:], lg[:])
                V.tensor_scalar(neg_g[:], gtop[:, 0:1], -1.0, None, ALU.mult)
                V.drain()
                V.tensor_copy(gidx_f[:], gidx[:, 0:1])
                V.drain()
                V.tensor_scalar(goh[:], iota[:, 0:NG], gidx_f[:], None, ALU.is_equal)
                V.tensor_scalar(gbase[:], gidx_f[:], float(EPG), None, ALU.mult)
                V.drain()
                V.tensor_tensor(lsel[:], le[:].rearrange("p (g e) -> p g e", g=NG),
                                goh[:].unsqueeze(2).to_broadcast((P, NG, EPG)), ALU.mult)
                V.drain()
                V.reduce_sum(esel[:], lsel[:].rearrange("p g e -> p e g"), axis=X)
                V.drain()
                V.max(etop[:], esel[:])
                V.drain()
                V.max_index(eidx[:], etop[:], esel[:])
                V.tensor_scalar(neg_e[:], etop[:, 0:1], -1.0, None, ALU.mult).then_inc(v_g, 1)
                V.drain()
                V.tensor_copy(eid[:], eidx[:, 0:2])
                V.drain()
                V.tensor_scalar(eid[:], eid[:], gbase[:], None, ALU.add)
                V.drain()
                V.tensor_tensor(oh[:], iota.unsqueeze(1).to_broadcast((P, 2, NE)),
                                eid[:].unsqueeze(2).to_broadcast((P, 2, NE)), ALU.is_equal)
                V.drain()
                V.tensor_tensor(oh_sum[:], oh[:, 0, :], oh[:, 1, :], ALU.add).then_inc(v_oh, 1)
                dve.wait_ge(a_ex, r + 1)
                V.tensor_scalar(wden[:], ed[:], 1.0, gsum[:], ALU.add, ALU.mult)
                V.drain()
                V.reciprocal(wts[:, 0:1], wden[:])
                V.drain()
                V.tensor_tensor(wts[:, 1:2], wts[:, 0:1], ed[:], ALU.mult)
                V.drain()

            def step(i):
                m, r, s = i - 1, i - 2, i - 3
                if within(i, 1, NT):
                    dve.wait_ge(pe_y, 2 * m + 2)
                    dve.wait_ge(ld_x, 16 * (m + 1))
                    after(dve, st_h, 16 * m)
                    V.tensor_tensor(h[:], ps_y[:], xt[:], ALU.add).then_inc(v_h, 1)
                if within(i, 1, NT - 1):
                    split_half(i, 1)
                if within(i, 3, NT + 2):
                    entries(s)
                if within(i, 1, NT):
                    dve.wait_ge(p_rstd, m + 1)
                    after(dve, st_hn, 16 * m)
                    after(dve, pe_ht, m)
                    V.scalar_tensor_tensor(hn[:], h[:], rstd[:], gffn[:], ALU.mult, ALU.mult).then_inc(v_hn, 1)
                if within(i, 0, NT - 2):
                    split_half(i + 1, 0)
                if within(i, 2, NT + 1):
                    route(r)

            V.memset(zero[:], 0.0)
            V.memset(lg[:], NEG)
            V.memset(oh_acc[:], 0.0)
            V.memset(entry[:], 0)
            for k in range(KT):
                j = k // 2
                dve.wait_ge(a_whi, k + 1)
                V.scalar_tensor_tensor(wo_lo[:, k, :], by_rows(shared.raw[j % RAW], D)[:, k % 2], gains[:, k:k + 1],
                                       wo_hi[:, k, :].bitcast(F32), ALU.mult, ALU.subtract).then_inc(v_wlo, 1)
                if k in (2, 4):
                    split_half(0, (k - 2) // 2)
            dve.wait_ge(ld_small, 16 * N_SMALL)
            V.tensor_copy(before[:], mats_sb[:, P:2 * P])
            V.tensor_copy(ones[:], mats_sb[:, 2 * P:3 * P])
            V.tensor_tensor(upto[:], mats_sb[:, P:P + NE], mats_sb[:, 0:NE], ALU.add)
            V.memset(bstart[:], 0)
            V.drain().then_inc(v_init, 1)
            all_steps(dve, step)
            V.drain().then_inc(v_acc, 1)
            dve.wait_ge(pe_cnt, 1)
            V.tensor_scalar(blocks[:], ps_k[0:NE, 0:1], float(BLK - 1), None, ALU.add)
            V.drain()
            V.tensor_copy(cnt_i[:], blocks[:])
            V.drain()
            V.tensor_scalar(cnt_i[:], cnt_i[:], 7, None, ALU.arith_shift_right)
            V.drain()
            V.tensor_copy(blocks[:], cnt_i[:])
            V.drain()
            V.tensor_scalar(blocks[:], blocks[:], 2.0, None, ALU.max).then_inc(v_blocks, 1)
            V.drain()
            V.tensor_scalar(skip[:], blocks[:], -float(BLK), float(ROWS_PER_EXPERT), ALU.mult, ALU.add)
            dve.wait_ge(pe_end, 1)
            V.tensor_copy(end[:], ps_k[0:NE, 1:2])
            V.drain()
            V.tensor_scalar(ended[:], iota_b[0:NE, :], end[:], None, ALU.is_ge).then_inc(v_ended, 1)
            V.tensor_copy(bstart[0:1, 1:NE + 1], ps_r[0:1, 0:NE])
            V.tensor_scalar(bstart[0:1, NE + 1:NE + 2], ps_r[0:1, NE - 1:NE], -1.0, None, ALU.add)
            dve.wait_ge(pe_row, 1)
            V.scalar_tensor_tensor(first_row[:], iota_b[0:1, :], float(BLK), ps_y[0:1, 0:MAXB], ALU.mult, ALU.add)
            V.drain()
            V.tensor_scalar(brow[:], first_row[:], float(NE * ROWS_PER_EXPERT - BLK), None, ALU.min)

        @block.gpsimd
        def _(pool):
            def step(i):
                m, s = i - 1, i - 3
                if within(i, 1, NT):
                    pool.wait_ge(a_hsq, m + 1)
                    after(pool, v_hn, m)
                    pool.sem_inc(p_held, 1)
                    nc.gpsimd.tensor_scalar(rstd[:], ssq[:], 1.0 / D, EPS, ALU.mult, ALU.add)
                    nc.gpsimd.drain()
                    nc.gpsimd.tensor_tensor(rstd[:], rstd[:], minus_half[:], ALU.pow).then_inc(p_rstd, 1)
                if within(i, 3, NT + 2):
                    pool.wait_ge(v_ent, s + 1)
                    pool.sem_inc(p_held, 1)
                    for k in range(2):
                        nc.gpsimd.indirect_dma_start(
                            out=table, out_offset=bass.IndirectOffsetOnAxis(ap=dest[:, k:k + 1], axis=0),
                            in_=entry[:, k, :], in_offset=None).then_inc(st_ent, 16)

            nc.gpsimd.memset(minus_half[:], -0.5)
            nc.gpsimd.drain()
            pool.wait_ge(shared.st_pad, 16)
            all_steps(pool, step)
            pool.wait_ge(st_ent, 32 * NT)


def experts(nc, shared, w_gate, w_up, w_down, hn_dram, h_dram, table, bstart, brow):
    with ExitStack() as ctx:
        sb, pb, sem = makers(ctx, nc, "experts")

        RING = 4
        we_hi = [sb(f"we_hi{p}", [P, CH, CW], F32R) for p in range(2)]
        we_lo = [sb(f"we_lo{p}", [P, CH, CW], BF16) for p in range(2)]
        raw = shared.raw
        ident = shared.ident
        ring = sb("ring", [P, RING, ENTRY], I32)
        row_in = sb("row_in", [P, ENTRY], I32)
        row_out = sb("row_out", [P, ENTRY], I32)
        xg = sb("xg", [P, D])
        xT_hi = sb("xT_hi", [P, KT, P], F32R)
        xT_lo = sb("xT_lo", [P, KT, P], F32R)
        xT_b = sb("xT_b", [P, KT, P], BF16)
        silu = sb("silu", [P, F])
        hid = sb("hid", [P, F])
        hT_hi = sb("hT_hi", [P, FT, P], F32R)
        hT_lo = sb("hT_lo", [P, FT, P], F32R)
        hT_b = sb("hT_b", [P, FT, P], BF16)
        y = sb("y", [P, D])

        ps_x = pb("ps_x", [P, KT, P])
        ps_g = pb("ps_g", [P, F])
        ps_u = pb("ps_u", [P, F])
        ps_h = pb("ps_h", [P, FT, P])
        ps_y = pb("ps_y", [P, D])

        ld_raw = shared.ld_exp
        ld_ring = sem("ld_ring")
        p_in = sem("p_in")
        p_out = sem("p_out")
        ld_x = sem("ld_x")
        st_y = sem("st_y")
        a_w = sem("a_w")
        v_w = sem("v_w")
        pe_xt = sem("pe_xt")
        pe_g = sem("pe_g")
        pe_u = sem("pe_u")
        pe_ht = sem("pe_ht")
        pe_dn = sem("pe_dn")
        a_sl = sem("a_sl")
        a_xh = sem("a_xh")
        a_hh = sem("a_hh")
        a_y = sem("a_y")
        v_hm = sem("v_hm")
        v_xl = sem("v_xl")
        v_hl = sem("v_hl")
        p_y = sem("p_y")
        held = {e: sem(f"held_{e}") for e in ("pe", "act", "pool")}

        block = ctx.enter_context(nc.Block())

        def bounds(engine, e):
            col = bass.ds(e, 1) if not isinstance(e, int) else slice(e, e + 1)
            nxt = bass.ds(e + 1, 1) if not isinstance(e, int) else slice(e + 1, e + 2)
            return (engine.value_load(bstart[0:1, col], min_val=0, max_val=MAXB - 4),
                    engine.value_load(bstart[0:1, nxt], min_val=2, max_val=MAXB - 2))

        def all_experts(engine, expert):
            expert(0, 0, True)
            expert(1, 1, True)
            with engine.Fori(1, NE // 2 - 1) as pair:
                expert(2 * pair, 0, True)
                expert(2 * pair + 1, 1, True)
            expert(NE - 2, 0, True)
            expert(NE - 1, 1, False)

        @block.sync
        def _(sp):
            def load_weights(e, first=0):
                for c in range(first, CH):
                    sp.wait_ge(v_w, CH * e + c + 1 - RAW)
                    sp.dma_start(by_rows(raw[c % RAW], F if c < 4 else D),
                                 expert_chunk(w_gate, w_up, w_down, c, e)).then_inc(ld_raw[c % RAW], 16)

            load_weights(0, RAW)
            with sp.Fori(1, NE) as e:
                load_weights(e)

        @block.tensor
        def _(pe):
            def x_transposes(n):
                pe.wait_ge(ld_x, 16 * (n + 1))
                for k in range(KT):
                    last = nc.tensor.transpose(ps_x[:, k, :], xg[:, k * P:(k + 1) * P], ident[:])
                last.then_inc(pe_xt, 1)

            def project_in(out, first_chunk, p):
                for k in range(KT):
                    cols = slice((k % 4) * F, (k % 4 + 1) * F)
                    c = first_chunk + k // 4
                    nc.tensor.matmul(out, xT_hi[:, k, :], we_hi[p][:, c, cols], start=(k == 0), stop=False)
                    nc.tensor.matmul(out, xT_lo[:, k, :], we_hi[p][:, c, cols], start=False, stop=False)
                    last = nc.tensor.matmul(out, xT_b[:, k, :], we_lo[p][:, c, cols], start=False, stop=(k == KT - 1))
                return last

            def down(g, p):
                pe.wait_ge(a_y, g + 1)
                pe.wait_ge(v_hl, g + 1)
                for half in range(2):
                    out = ps_y[:, half * 512:(half + 1) * 512]
                    for k in range(FT):
                        c, a = 4 + k // 2, (k % 2) * D + half * 512
                        nc.tensor.matmul(out, hT_hi[:, k, :], we_hi[p][:, c, a:a + 512], start=(k == 0), stop=False)
                        nc.tensor.matmul(out, hT_lo[:, k, :], we_hi[p][:, c, a:a + 512], start=False, stop=False)
                        last = nc.tensor.matmul(out, hT_b[:, k, :], we_lo[p][:, c, a:a + 512], start=False, stop=(k == FT - 1))
                last.then_inc(pe_dn, 1)

            def run_block(g, p, down_p, e=None):
                pe.wait_ge(v_xl, g + 1)
                if e is not None:
                    pe.wait_ge(v_w, CH * e + 2)
                project_in(ps_g[:], 0, p).then_inc(pe_g, 1)
                if e is not None:
                    pe.wait_ge(v_w, CH * e + 4)
                project_in(ps_u[:], 2, p).then_inc(pe_u, 1)
                x_transposes(g + 1)
                if down_p is not None:
                    down(g - 1, down_p)
                pe.wait_ge(v_hm, g + 1)
                for k in range(FT):
                    last = nc.tensor.transpose(ps_h[:, k, :], hid[:, k * P:(k + 1) * P], ident[:])
                last.then_inc(pe_ht, 1)

            def expert(e, p, prefetch):
                g0, g1 = bounds(pe, e)
                run_block(g0, p, None if isinstance(e, int) and e == 0 else 1 - p, e)
                pe.wait_ge(v_w, CH * (e + 1))
                pe.sem_inc(held["pe"], 1)
                run_block(g0 + 1, p, p)
                with pe.If_lt(pe.to_reg(g0 + 2), g1):
                    with pe.Fori(g0 + 2, g1) as g:
                        run_block(g, p, p)

            pe.sem_inc(pe_dn, 1)
            x_transposes(0)
            all_experts(pe, expert)
            down(pe.value_load(bstart[0:1, NE:NE + 1], min_val=2, max_val=MAXB - 2) - 1, 1)

        @block.scalar
        def _(act):
            def split_weights(e, c, p):
                act.wait_ge(ld_raw[c % RAW], 16 * (2 * e + c // RAW + 1))
                nc.scalar.copy(we_hi[p][:, c, :], raw[c % RAW][:]).then_inc(a_w, 1)

            def split_x(n):
                act.wait_ge(pe_xt, n + 1)
                nc.scalar.copy(xT_hi[:], ps_x[:]).then_inc(a_xh, 1)

            def weigh(g):
                act.wait_ge(pe_dn, g + 2)
                act.wait_ge(p_out, g + 1)
                act.wait_ge(p_y, g + 1)
                act.sem_inc(held["act"], 1)
                nc.scalar.mul(y[:], ps_y[:], row_out[:, 2:3].bitcast(F32)).then_inc(a_y, 1)

            def run_block(g, weights, first=False):
                if not first:
                    weights(0)
                act.wait_ge(pe_g, g + 1)
                nc.scalar.activation(silu[:], ps_g[:], ACT.Silu).then_inc(a_sl, 1)
                if not first:
                    weights(1)
                split_x(g + 1)
                if first:
                    weights(0)
                    weights(1)
                else:
                    weigh(g - 1)
                act.wait_ge(pe_ht, g + 1)
                nc.scalar.copy(hT_hi[:], ps_h[:]).then_inc(a_hh, 1)
                weights(2)

            def expert(e, p, prefetch):
                g0, g1 = bounds(act, e)
                split = (lambda c: split_weights(e + 1, c, 1 - p)) if prefetch else (lambda c: None)
                run_block(g0, split, isinstance(e, int) and e == 0)
                run_block(g0 + 1, lambda n: split(CH // 2 + n))
                with act.If_lt(act.to_reg(g0 + 2), g1):
                    with act.Fori(g0 + 2, g1) as g:
                        run_block(g, lambda n: None)

            act.sem_inc(a_y, 1)
            for c in range(CH):
                split_weights(0, c, 0)
                if c == RAW - 1:
                    split_x(0)
            all_experts(act, expert)
            weigh(act.value_load(bstart[0:1, NE:NE + 1], min_val=2, max_val=MAXB - 2) - 1)

        @block.vector
        def _(dve):
            V = nc.vector

            def split_weights(e, c, p):
                dve.wait_ge(a_w, CH * e + c + 1)
                V.tensor_tensor(we_lo[p][:, c, :], raw[c % RAW][:], we_hi[p][:, c, :].bitcast(F32), ALU.subtract).then_inc(v_w, 1)

            def split_x(n):
                dve.wait_ge(a_xh, n + 1)
                V.tensor_copy(xT_b[:], xT_hi[:].bitcast(F32))
                V.tensor_tensor(xT_lo[:], ps_x[:], xT_hi[:].bitcast(F32), ALU.subtract).then_inc(v_xl, 1)

            def run_block(g, weights, first=False):
                if not first:
                    weights(0)
                dve.wait_ge(pe_u, g + 1)
                dve.wait_ge(a_sl, g + 1)
                V.tensor_tensor(hid[:], silu[:], ps_u[:], ALU.mult).then_inc(v_hm, 1)
                if not first:
                    weights(1)
                split_x(g + 1)
                if first:
                    weights(0)
                    weights(1)
                dve.wait_ge(a_hh, g + 1)
                V.tensor_copy(hT_b[:], hT_hi[:].bitcast(F32))
                V.tensor_tensor(hT_lo[:], ps_h[:], hT_hi[:].bitcast(F32), ALU.subtract).then_inc(v_hl, 1)
                weights(2)

            def expert(e, p, prefetch):
                g0, g1 = bounds(dve, e)
                split = (lambda c: split_weights(e + 1, c, 1 - p)) if prefetch else (lambda c: None)
                run_block(g0, split, isinstance(e, int) and e == 0)
                run_block(g0 + 1, lambda n: split(CH // 2 + n))
                with dve.If_lt(dve.to_reg(g0 + 2), g1):
                    with dve.Fori(g0 + 2, g1) as g:
                        run_block(g, lambda n: None)

            for c in range(CH):
                split_weights(0, c, 0)
                if c == RAW - 1:
                    split_x(0)
            all_experts(dve, expert)

        @block.gpsimd
        def _(pool):
            def load_ring(g):
                row = pool.value_load(brow[0:1, bass.ds(g, 1)], min_val=0, max_val=NE * ROWS_PER_EXPERT - BLK)
                pool.dma_start(ring[:, bass.ds(g & (RING - 1), 1), :].rearrange("p a c -> p (a c)"),
                               table[bass.ds(row, BLK), :]).then_inc(ld_ring, 16)

            def gather(g):
                pool.wait_ge(ld_ring, 16 * (g + 1))
                pool.sem_inc(held["pool"], 1)
                nc.gpsimd.tensor_copy(row_in[:], ring[:, bass.ds(g & (RING - 1), 1), :].rearrange("p a c -> p (a c)")).then_inc(p_in, 1)
                pool.wait_ge(p_in, g + 1)
                pool.sem_inc(held["pool"], 1)
                nc.gpsimd.indirect_dma_start(out=xg[:], out_offset=None, in_=hn_dram,
                                             in_offset=bass.IndirectOffsetOnAxis(ap=row_in[:, 0:1], axis=0)).then_inc(ld_x, 16)

            def rows_out(g):
                nc.gpsimd.tensor_copy(row_out[:], ring[:, bass.ds(g & (RING - 1), 1), :].rearrange("p a c -> p (a c)")).then_inc(p_out, 1)

            def add_rows(n):
                pool.wait_ge(a_y, n + 1)
                pool.wait_ge(p_out, n)
                pool.sem_inc(held["pool"], 1)
                nc.gpsimd.indirect_dma_start(out=h_dram, out_offset=bass.IndirectOffsetOnAxis(ap=row_out[:, 1:2], axis=0),
                                             in_=y[:], in_offset=None, compute_op=ALU.add).then_inc(st_y, 16)
                pool.wait_ge(st_y, 16 * n)
                pool.sem_inc(p_y, 1)

            def step(g, first=0):
                pool.wait_ge(pe_xt, g + 1)
                gather(g + 1)
                load_ring(g + 2)
                if first < 1:
                    add_rows(g - 1)
                if first < 2:
                    rows_out(g - 1)

            pool.sem_inc(p_y, 1)
            load_ring(0)
            gather(0)
            load_ring(1)
            step(0, 2)
            step(1, 1)
            total = pool.value_load(bstart[0:1, NE:NE + 1], min_val=2, max_val=MAXB - 2)
            with pool.Fori(2, total) as g:
                step(g)
            last = pool.value_load(bstart[0:1, NE + 1:NE + 2], min_val=1, max_val=MAXB - 3)
            add_rows(last)
            rows_out(last)
            add_rows(total)
            pool.wait_ge(ld_ring, 16 * (total + 2))
            pool.wait_ge(ld_x, 16 * (total + 1))


def final(nc, h_dram, g_final, out):
    SLOTS = 4
    with ExitStack() as ctx:
        sb, pb, sem = makers(ctx, nc, "final")
        gain = sb("gain", [P, D])
        h = [sb(f"hf{s}", [P, D]) for s in range(SLOTS)]
        o = [sb(f"of{s}", [P, D]) for s in range(SLOTS)]
        junk = [sb(f"junk{s}", [P, D]) for s in range(SLOTS)]
        ssq = [sb(f"ssq{s}", [P, 1]) for s in range(SLOTS)]
        rstd = [sb(f"rstd{s}", [P, 1]) for s in range(SLOTS)]
        minus_half = sb("minus_half", [P, 1])
        ld_g = sem("ld_g")
        ld_h = [sem(f"ld_h{s}") for s in range(SLOTS)]
        st_o = [sem(f"st_o{s}") for s in range(SLOTS)]
        a_sq = sem("a_sq")
        p_rs = sem("p_rs")
        p_held = sem("p_held")
        v_o = sem("v_o")
        h_t = h_dram.rearrange("(t p) d -> t p d", p=P)
        out_t = out.rearrange("b (t p) d -> (b t) p d", p=P)
        block = ctx.enter_context(nc.Block())

        def rounds(engine, tile):
            for s in range(SLOTS):
                tile(0, s)
            with engine.Fori(1, NT // SLOTS) as r:
                for s in range(SLOTS):
                    tile(r, s)

        @block.sync
        def _(sp):
            def tile(r, s):
                after(sp, v_o, SLOTS * (r - 1) + s + 1)
                sp.dma_start(h[s][:], h_t[bass.ds(SLOTS * r + s, 1)].rearrange("a p d -> (a p) d")).then_inc(ld_h[s], 16)
                if isinstance(r, int) and s == 0:
                    sp.dma_start(gain[:], g_final.rearrange("(a d) -> a d", a=1).to_broadcast((P, D))).then_inc(ld_g, 16)

            rounds(sp, tile)

        @block.scalar
        def _(act):
            def tile(r, s):
                act.wait_ge(ld_h[s], 16 * (r + 1))
                after(act, p_rs, SLOTS * (r - 1) + s + 1)
                nc.scalar.activation(junk[s][:], h[s][:], ACT.Square, accum_out=ssq[s][:]).then_inc(a_sq, 1)
                if not (isinstance(r, int) and s == 0):
                    store(SLOTS * r + s - 1, r if s else r - 1, (s - 1) % SLOTS)

            def store(n, r, s):
                act.wait_ge(v_o, n + 1)
                act.dma_start(out_t[bass.ds(n, 1)].rearrange("a p d -> (a p) d"), o[s][:]).then_inc(st_o[s], 16)

            rounds(act, tile)
            store(NT - 1, NT // SLOTS - 1, SLOTS - 1)
            for s in range(SLOTS):
                act.wait_ge(st_o[s], 16 * (NT // SLOTS))

        @block.gpsimd
        def _(pool):
            nc.gpsimd.memset(minus_half[:], -0.5)
            nc.gpsimd.drain()

            def tile(r, s):
                pool.wait_ge(a_sq, SLOTS * r + s + 1)
                after(pool, v_o, SLOTS * (r - 1) + s + 1)
                pool.sem_inc(p_held, 1)
                nc.gpsimd.tensor_scalar(rstd[s][:], ssq[s][:], 1.0 / D, EPS, ALU.mult, ALU.add)
                nc.gpsimd.drain()
                nc.gpsimd.tensor_tensor(rstd[s][:], rstd[s][:], minus_half[:], ALU.pow).then_inc(p_rs, 1)

            rounds(pool, tile)

        @block.vector
        def _(dve):
            dve.wait_ge(ld_g, 16)

            def tile(r, s):
                dve.wait_ge(p_rs, SLOTS * r + s + 1)
                after(dve, st_o[s], 16 * r)
                nc.vector.scalar_tensor_tensor(o[s][:], h[s][:], rstd[s][:], gain[:], ALU.mult, ALU.mult).then_inc(v_o, 1)

            rounds(dve, tile)


def build(nc, a, out):
    mix_dram = nc.dram_tensor("mix_rows", (SEQ, D), F32, kind="Internal").ap()
    h_dram = nc.dram_tensor("h_rows", (SEQ + P, D), F32, kind="Internal").ap()
    hn_dram = nc.dram_tensor("hn_rows", (SEQ, D), F32, kind="Internal").ap()
    table = nc.dram_tensor("expert_rows", (NE * ROWS_PER_EXPERT, ENTRY), I32, kind="Internal").ap()
    with ExitStack() as ctx:
        shared = Shared(ctx, nc)
        bstart = ctx.enter_context(nc.sbuf_tensor("bstart", [1, NE + 2], I32))
        brow = ctx.enter_context(nc.sbuf_tensor("brow", [1, MAXB], I32))
        mixers(nc, shared, a["x"], a["w_in"], a["b_in"], a["sinks"], a["gmlp_w_s"], a["gmlp_b_s"], a["gmlp_ln_g"],
               a["gmlp_ln_b"], a["g_mix_norm"], a["w_out"], a["mats"], a["pad"], a["rope"], mix_dram, table)
        project(nc, shared, a["x"], mix_dram, a["w_out"], a["g_attn_out"], a["g_gmlp_out"], a["g_ffn_norm"],
                a["w_router_group"], a["b_router_group"], a["w_router_expert"], a["b_router_expert"],
                a["mats"], a["toks"], a["w_gate"], a["w_up"], a["w_down"], h_dram, hn_dram, table, bstart, brow)
        experts(nc, shared, a["w_gate"], a["w_up"], a["w_down"], hn_dram, h_dram, table, bstart, brow)
        final(nc, h_dram, a["g_final"], out)


def shape_constants():
    mats = np.zeros((P, 3 * P + MAXB), np.float32)
    mats[:, 0:P] = np.eye(P)
    mats[:, P:2 * P] = np.triu(np.ones((P, P)), 1)
    mats[:, 2 * P:3 * P] = 1.0
    mats[:, 3 * P:] = np.arange(MAXB)
    inv = np.float32(500000.0) ** (-np.arange(0, ROT, 2, dtype=np.float32) / np.float32(ROT))
    ang = np.arange(SEQ, dtype=np.float32)[:, None] * inv[None, :]
    cos, sin = np.cos(ang), np.sin(ang)
    rope = np.concatenate([cos, cos, -sin, sin], 1).astype(np.float32)
    toks = (np.arange(P)[:, None] + P * np.arange(NT)[None, :]).astype(np.int32)
    rows = np.arange(NE * ROWS_PER_EXPERT)
    pad = np.zeros((NE * ROWS_PER_EXPERT, ENTRY), np.int32)
    pad[:, 0] = rows % P
    pad[:, 1] = SEQ + rows % P
    return {"mats": mats, "rope": rope, "toks": toks, "pad": pad}


_INS = ["x", "g_mix_norm", "w_in", "b_in", "sinks", "gmlp_w_s", "gmlp_b_s", "gmlp_ln_g", "gmlp_ln_b", "g_attn_out",
        "g_gmlp_out", "w_out", "g_ffn_norm", "w_router_group", "b_router_group", "w_router_expert",
        "b_router_expert", "w_gate", "w_up", "w_down", "g_final"]


def kernel(**inputs):
    import concourse.bacc as bacc
    from concourse.bass_utils import run_bass_kernel_spmd

    nc = bacc.Bacc("TRN2", target_bir_lowering=False, num_devices=1)
    arrays, aps = {}, {}
    for name, value in [(n, inputs[n]) for n in _INS] + list(shape_constants().items()):
        value = np.ascontiguousarray(value)
        arrays[f"in_{name}"] = value
        aps[name] = nc.dram_tensor(f"in_{name}", value.shape, mybir.dt.from_np(value.dtype), kind="ExternalInput").ap()
    out = nc.dram_tensor("out", (1, SEQ, D), F32, kind="ExternalOutput").ap()
    build(nc, aps, out)
    result = run_bass_kernel_spmd(nc, [arrays], core_ids=[0])
    return result.results[0]["out"]
```
